# Optimizing a Trainium2 kernel written in Bass

```python
import math
import jax, jax.numpy as jnp
from jax import lax
import numpy as np

D_MODEL = 1024
BATCH = 1
SEQ = 256
DEPTH = 2

EPS = 1e-6
MIX_DIM = D_MODEL
CONV_DIM = MIX_DIM // 2
CONV_GROUPS = 8
CONV_K = 3
LSTM_HEADS = 4
LSTM_DIM = MIX_DIM - CONV_DIM
LSTM_DH = LSTM_DIM // LSTM_HEADS
CHUNK = 128
OFF_XIN = 0
OFF_B = OFF_XIN + CONV_DIM
OFF_C = OFF_B + CONV_DIM
OFF_Q = OFF_C + CONV_DIM
OFF_K = OFF_Q + LSTM_DIM
OFF_V = OFF_K + LSTM_DIM
OFF_O = OFF_V + LSTM_DIM
OFF_IF = OFF_O + LSTM_DIM
IN_COLS = OFF_IF + 2 * LSTM_HEADS
N_MEM = 256
X_HEADS = 4
X_DH = D_MODEL // X_HEADS
P_HEADS = 8
N_KEYS = 128
N_EXPERTS = N_KEYS * N_KEYS
P_QDIM = 256
P_HALF = P_QDIM // 2
TOPK = 16
PEER_BLOCK = 128

kernel_name = 'hybrid_conv_mlstm_peer_block'

def rms_norm(x, g):
    xf = x.astype(jnp.float32)
    y = xf * lax.rsqrt(jnp.mean(xf * xf, axis=-1, keepdims=True) + EPS)
    return (y * g.astype(jnp.float32)).astype(x.dtype)

def mlstm_chunkwise(q, k, v, i_pre, f_pre):
    B, S, H, DH = q.shape
    NC = S // CHUNK
    f32 = jnp.float32

    def to_chunks(a):
        return a.astype(f32).reshape(B, NC, CHUNK, H, DH).transpose(1, 0, 3, 2, 4)

    def gate_chunks(a):
        return a.astype(f32).reshape(B, NC, CHUNK, H).transpose(1, 0, 3, 2)

    qc = to_chunks(q)
    kc = to_chunks(k) * (DH ** -0.5)
    vc = to_chunks(v)
    ig = gate_chunks(i_pre)
    bcum = jnp.cumsum(jax.nn.log_sigmoid(gate_chunks(f_pre)), axis=-1)
    mask = jnp.tril(jnp.ones((CHUNK, CHUNK), dtype=bool))

    def step(carry, inp):
        C, n, m = carry
        q_, k_, v_, i_, b_ = inp
        D = b_[..., :, None] - b_[..., None, :] + i_[..., None, :]
        D = jnp.where(mask, D, -jnp.inf)
        inter = b_ + m[..., None]
        m_t = jnp.maximum(inter, jnp.max(D, axis=-1))
        Dw = jnp.exp(D - m_t[..., None])
        iw = jnp.exp(inter - m_t)
        s = jnp.einsum('bhtd,bhsd->bhts', q_, k_) * Dw
        num = jnp.einsum('bhts,bhsv->bhtv', s, v_) + iw[..., None] * jnp.einsum('bhvk,bhtk->bhtv', C, q_)
        den = jnp.sum(s, axis=-1) + iw * jnp.einsum('bhtk,bhk->bht', q_, n)
        h = num / jnp.maximum(jnp.abs(den), jnp.exp(-m_t))[..., None]
        bL = b_[..., -1]
        gsum = bL[..., None] - b_ + i_
        m_new = jnp.maximum(bL + m, jnp.max(gsum, axis=-1))
        wdec = jnp.exp(bL + m - m_new)
        ws = jnp.exp(gsum - m_new[..., None])
        C_new = wdec[..., None, None] * C + jnp.einsum('bhsv,bhsk->bhvk', v_ * ws[..., None], k_)
        n_new = wdec[..., None] * n + jnp.einsum('bhs,bhsk->bhk', ws, k_)
        return (C_new, n_new, m_new), h

    init = (jnp.zeros((B, H, DH, DH), f32), jnp.zeros((B, H, DH), f32), jnp.zeros((B, H), f32))
    _, hs = lax.scan(step, init, (qc, kc, vc, ig, bcum))
    return hs.transpose(1, 0, 3, 2, 4).reshape(B, S, H, DH)

def hybrid_mixer(h, w_in, b_if, conv_w, conv_b, g_head, w_out):
    B, S, _ = h.shape
    z = h @ w_in
    xin = z[..., OFF_XIN:OFF_B]
    bg = z[..., OFF_B:OFF_C]
    cg = z[..., OFF_C:OFF_Q]
    q = z[..., OFF_Q:OFF_K].reshape(B, S, LSTM_HEADS, LSTM_DH)
    k = z[..., OFF_K:OFF_V].reshape(B, S, LSTM_HEADS, LSTM_DH)
    v = z[..., OFF_V:OFF_O].reshape(B, S, LSTM_HEADS, LSTM_DH)
    o = jax.nn.sigmoid(z[..., OFF_O:OFF_IF])
    gates = z[..., OFF_IF:] + b_if
    i_pre = gates[..., :LSTM_HEADS]
    f_pre = gates[..., LSTM_HEADS:]

    u = cg * xin
    c = lax.conv_general_dilated(u, conv_w[:, None, :], window_strides=(1,), padding=[(CONV_K - 1, 0)],
                                 dimension_numbers=('NWC', 'WIO', 'NWC'), feature_group_count=CONV_DIM)
    y_conv = bg * (c + conv_b)

    ht = mlstm_chunkwise(q, k, v, i_pre, f_pre).reshape(B, S, LSTM_DIM)
    hl = (o.astype(jnp.float32) * ht).reshape(B, S, LSTM_HEADS, LSTM_DH)
    hl = hl * lax.rsqrt(jnp.mean(hl * hl, axis=-1, keepdims=True) + EPS)
    y_lstm = (hl.reshape(B, S, LSTM_DIM) * g_head.astype(jnp.float32)).astype(h.dtype)

    return jnp.concatenate([y_conv, y_lstm], axis=-1) @ w_out

def memory_cross_attention(h, memn, w_xq, w_xk, w_xv, w_xo):
    B, S, _ = h.shape
    q = (h @ w_xq).reshape(B, S, X_HEADS, X_DH)
    k = (memn @ w_xk).reshape(B, N_MEM, X_HEADS, X_DH)
    v = (memn @ w_xv).reshape(B, N_MEM, X_HEADS, X_DH)
    s = jnp.einsum('bshd,bmhd->bhsm', q, k).astype(jnp.float32) * (X_DH ** -0.5)
    p = jax.nn.softmax(s, axis=-1).astype(h.dtype)
    out = jnp.einsum('bhsm,bmhd->bshd', p, v).reshape(B, S, D_MODEL)
    return out @ w_xo

def peer_ffn(h, w_pq, sub_keys, u_experts, v_experts):
    B, S, D = h.shape
    blocks = h.reshape(-1, PEER_BLOCK, D)

    def block(xb):
        q = (xb @ w_pq).reshape(PEER_BLOCK, P_HEADS, 2, P_HALF)
        sc = jnp.einsum('thpc,hpkc->thpk', q, sub_keys)
        sv, si = lax.top_k(sc, TOPK)
        cand = (sv[..., 0, :, None] + sv[..., 1, None, :]).reshape(PEER_BLOCK, P_HEADS, TOPK * TOPK)
        cid = (si[..., 0, :, None] * N_KEYS + si[..., 1, None, :]).reshape(PEER_BLOCK, P_HEADS, TOPK * TOPK)
        fv, fi = lax.top_k(cand, TOPK)
        eid = jnp.take_along_axis(cid, fi, axis=-1)
        g = jax.nn.softmax(fv.astype(jnp.float32), axis=-1).astype(xb.dtype)
        ue = jnp.take(u_experts, eid, axis=0)
        ve = jnp.take(v_experts, eid, axis=0)
        a = jax.nn.gelu(jnp.einsum('thkd,td->thk', ue, xb), approximate=False)
        return jnp.einsum('thk,thkd->td', g * a, ve)

    return lax.map(block, blocks).reshape(B, S, D)

def setup_inputs(seed: int = 0) -> dict:
    key = jax.random.key(seed)
    ks = jax.random.split(key, 24)

    def nrm(k, shape, scale):
        return jax.random.normal(k, shape, jnp.float32) * scale

    x = nrm(ks[0], (BATCH, SEQ, D_MODEL), 1.0)
    mem = nrm(ks[1], (BATCH, N_MEM, D_MODEL), 1.0)
    g_mix = 1.0 + nrm(ks[2], (DEPTH, D_MODEL), 0.02)
    w_in = nrm(ks[3], (DEPTH, D_MODEL, IN_COLS), D_MODEL ** -0.5)
    b_i = nrm(ks[4], (DEPTH, LSTM_HEADS), 0.1)
    b_f = 3.0 + nrm(ks[5], (DEPTH, LSTM_HEADS), 0.1)
    b_if = jnp.concatenate([b_i, b_f], axis=-1)
    conv_w = nrm(ks[6], (DEPTH, CONV_K, CONV_DIM), CONV_K ** -0.5)
    conv_b = nrm(ks[7], (DEPTH, CONV_DIM), 0.02)
    g_head = 1.0 + nrm(ks[8], (DEPTH, LSTM_DIM), 0.02)
    w_out = nrm(ks[9], (DEPTH, MIX_DIM, D_MODEL), MIX_DIM ** -0.5)
    g_xattn = 1.0 + nrm(ks[10], (DEPTH, D_MODEL), 0.02)
    g_mem = 1.0 + nrm(ks[11], (DEPTH, D_MODEL), 0.02)
    w_xq = nrm(ks[12], (DEPTH, D_MODEL, D_MODEL), D_MODEL ** -0.5)
    w_xk = nrm(ks[13], (DEPTH, D_MODEL, D_MODEL), D_MODEL ** -0.5)
    w_xv = nrm(ks[14], (DEPTH, D_MODEL, D_MODEL), D_MODEL ** -0.5)
    w_xo = nrm(ks[15], (DEPTH, D_MODEL, D_MODEL), D_MODEL ** -0.5)
    g_ffn = 1.0 + nrm(ks[16], (DEPTH, D_MODEL), 0.02)
    w_pq = nrm(ks[17], (DEPTH, D_MODEL, P_HEADS * P_QDIM), D_MODEL ** -0.5)
    sub_keys = nrm(ks[18], (DEPTH, P_HEADS, 2, N_KEYS, P_HALF), P_HALF ** -0.5)
    u_experts = nrm(ks[19], (DEPTH, N_EXPERTS, D_MODEL), D_MODEL ** -0.5)
    v_experts = nrm(ks[20], (DEPTH, N_EXPERTS, D_MODEL), 0.25)
    g_final = 1.0 + nrm(ks[21], (D_MODEL,), 0.02)
    return {'x': x, 'mem': mem, 'g_mix': g_mix, 'w_in': w_in, 'b_if': b_if, 'conv_w': conv_w,
            'conv_b': conv_b, 'g_head': g_head, 'w_out': w_out, 'g_xattn': g_xattn, 'g_mem': g_mem,
            'w_xq': w_xq, 'w_xk': w_xk, 'w_xv': w_xv, 'w_xo': w_xo, 'g_ffn': g_ffn, 'w_pq': w_pq,
            'sub_keys': sub_keys, 'u_experts': u_experts, 'v_experts': v_experts, 'g_final': g_final}

def reference(x, mem, g_mix, w_in, b_if, conv_w, conv_b, g_head, w_out, g_xattn, g_mem,
              w_xq, w_xk, w_xv, w_xo, g_ffn, w_pq, sub_keys, u_experts, v_experts, g_final):
    for l in range(DEPTH):
        h = rms_norm(x, g_mix[l])
        x = x + hybrid_mixer(h, w_in[l], b_if[l], conv_w[l], conv_b[l], g_head[l], w_out[l])
        h = rms_norm(x, g_xattn[l])
        x = x + memory_cross_attention(h, rms_norm(mem, g_mem[l]), w_xq[l], w_xk[l], w_xv[l], w_xo[l])
        h = rms_norm(x, g_ffn[l])
        x = x + peer_ffn(h, w_pq[l], sub_keys[l], u_experts[l], v_experts[l])
    return rms_norm(x, g_final)


_drawn_inputs = setup_inputs


def setup_inputs(seed=0):
    import zlib

    import numpy as np

    out = dict(_drawn_inputs(seed))
    spreads = {}
    factors = {'g_xattn': 7.31, 'g_mem': 5.779, 'g_final': 7.542, 'g_ffn': 3.146}
    for name, (base, spread) in spreads.items():
        noise = np.random.default_rng([zlib.crc32(name.encode()), seed]).standard_normal(out[name].shape)
        drawn = base * np.exp(spread * noise) if base else spread * noise
        out[name] = __import__('jax').numpy.asarray(drawn.astype(out[name].dtype))
    for name, factor in factors.items():
        out[name] = (out[name] * factor).astype(out[name].dtype)
    return out
```

```python
from contextlib import ExitStack

import concourse.bass as bass
from concourse import mybir

FP32 = mybir.dt.float32
F32R = mybir.dt.float32r
U32 = mybir.dt.uint32
ALU = mybir.AluOpType
ACT = mybir.ActivationFunctionType
AX = mybir.AxisListType
ds = bass.ds

P = 128
D = 1024
KB = D // P
T = 256
TB = T // P
NMEM = 256
DEPTH = 2
EPS = 1e-6
LH = 4
LSTM_SCALE = 128 ** -0.5
XH = 4
X_SCALE = 256 ** -0.5
PH = 8
SETS = 2 * PH
TOPK = 16
NKEYS = 128
LOWEST = -3.4028234663852886e38

IN_SLABS, KV_SLABS, OUT_SLABS, Q_SLABS, XO_SLABS, PQ_SLABS = 28, 16, 8, 8, 8, 16
U_SLABS = V_SLABS = 128
IN_AT = 0
KV_AT = IN_AT + IN_SLABS
OUT_AT = KV_AT + KV_SLABS
Q_AT = OUT_AT + OUT_SLABS
XO_AT = Q_AT + Q_SLABS
PQ_AT = XO_AT + XO_SLABS
U_AT = PQ_AT + PQ_SLABS
V_AT = U_AT + U_SLABS
SLABS = V_AT + V_SLABS
RING = 4
IN_EV, KV_EV = 0, IN_SLABS
Q_EV = KV_EV + KV_SLABS
PQ_EV = Q_EV + Q_SLABS
U_EV = PQ_EV + PQ_SLABS
ACT_EVS = U_EV + U_SLABS
DVE_EVS = OUT_SLABS + XO_SLABS

G_MIX, G_MEM, G_XATTN, G_FFN = 0, 8, 16, 24
G_HEAD, CONV_W, CONV_B, B_IF, W_IF = 32, 36, 48, 52, 60
N_PARAM = W_IF + KB * 8

USE_MIX, USE_MEM, USE_Y, USE_XATTN, USE_AO, USE_FFN, USES = range(7)
NORM_MIX, NORM_MEM, NORM_XATTN, NORM_FFN, NORMS = range(5)

KEYS_READ = 64
RETRIEVED = 88
POOL_TOKENS = (3, 2, 3, 2)
GROUPS = T // 4


class Steps:

    def __init__(self, eng, sem):
        self.eng, self.sem, self.n = eng, sem, 0

    def mark(self, ins):
        ins.then_inc(self.sem, 1)
        self.n += 1

    def join(self):
        self.eng.wait_ge(self.sem, self.n)

    def link(self, ins):
        self.mark(ins)
        self.join()

    def restart(self):
        self.join()
        self.eng.sem_clear(self.sem)
        self.n = 0


def trunk(nc, x, mem, slabs, params, g_final, sub_keys, out):
    ctx = ExitStack()
    with ctx:
        base = (nc.sbuf_base + 63) // 64 * 64
        limit = nc.sbuf_usable_end
        ctx.enter_context(nc.sbuf_tensor("arena", [P, (limit - base - 64) // 4], FP32))
        top = [base]

        def at(name, offset, shape, dt=FP32):
            return nc.alloc_sbuf_tensor_at(name, shape, dt, offset=offset)

        def sb(name, shape, dt=FP32):
            size = 4
            for n in shape[1:]:
                size *= n
            t = at(name, top[0], shape, dt)
            top[0] += (size + 31) // 32 * 32
            assert top[0] <= limit, name
            return t

        raw = sb("raw", [P, RING, D])
        w_hi = sb("w_hi", [P, RING, KB, P], F32R)
        w_lo = sb("w_lo", [P, RING, KB, P], F32R)
        xT = sb("xT", [P, KB, T])
        act_at = top[0]
        act_hi = sb("act_hi", [P, KB, T], F32R)
        act_lo = sb("act_lo", [P, KB, T], F32R)
        hot_col = at("hot_col", act_at, [P, RING, 4, P])
        y_nat = at("y_nat", act_at, [P, 4, 512])
        hot_row = at("hot_row", act_at + RING * 4 * P * 4, [P, RING, 4, P])
        ident = sb("ident", [P, P])
        eps = sb("eps", [P, 1])
        ones = sb("ones", [P, P])
        tri = sb("tri", [P, P])
        iota = sb("iota", [P, P])
        par = sb("par", [P, N_PARAM])
        gfin = sb("gfin", [P, KB])
        wif_hi = sb("wif_hi", [P, KB, 8], F32R)
        wif_lo = sb("wif_lo", [P, KB, 8], F32R)
        rowT = sb("rowT", [P, T])
        colT = sb("colT", [P, T])
        gateT = sb("gateT", [P, T])
        cols16 = sb("cols16", [P, 4 * RING])
        gated_at = top[0]
        gated = sb("gated", [P, NKEYS, T])

        def tmp(name, kib, shape, dt=FP32):
            size = 4
            for n in shape[1:]:
                size *= n
            assert kib * 1024 + size <= NKEYS * T * 4, name
            return at(name, gated_at + int(kib * 1024), shape, dt)

        memT = tmp("memT", 0, [P, KB, NMEM])
        kvT = tmp("kvT", 8, [P, KV_SLABS, NMEM])
        v_mem = tmp("v_mem", 24, [P, 2, D])
        zT = tmp("zT", 32, [P, IN_SLABS, T])
        u_pad = tmp("u_pad", 60, [P, 4, T + 2])
        conv = tmp("conv", 65, [P, 4, T])
        v_nat = tmp("v_nat", 69, [P, TB, LH, P])
        arg = tmp("arg", 73, [P, LH, 384])
        s_w = tmp("s_w", 79, [P, LH, 384])
        den = tmp("den", 85, [P, LH, T])
        hl = tmp("hl", 89, [P, LH, T])
        o_sig = tmp("o_sig", 93, [P, LH, T])
        gates = tmp("gates", 97, [P, TB, 8])
        nf = tmp("nf", 97.25, [P, TB, 4])
        ef = tmp("ef", 97.5, [P, TB, 4])
        ls = tmp("ls", 97.75, [P, TB, 4])
        b_nat = tmp("b_nat", 98, [P, TB, 4])
        r_nat = tmp("r_nat", 98.25, [P, TB, 4])
        mf = tmp("mf", 98.5, [P, TB, 4])
        r_row = tmp("r_row", 99, [4, T])
        m_row = tmp("m_row", 100, [4, T])
        e_row = tmp("e_row", 101, [4, T])
        rstd = tmp("rstd", 102, [P, T])
        sq = tmp("sq", 104, [P, KB, T])
        xn = tmp("xn", 112, [P, KB, T])
        skT = tmp("skT", 120, [P, SETS, NKEYS])
        qT = tmp("qT", 32, [P, KB, T])
        prob = tmp("prob", 40, [P, 2 * XH, NMEM])
        probT = tmp("probT", 48, [P, 2, XH, T])
        rmax = tmp("rmax", 97, [P, 8])
        nmax = tmp("nmax", 97.25, [P, 8])
        rsum = tmp("rsum", 97.5, [P, 8])
        rinv = tmp("rinv", 97.75, [P, 8])
        qpT = tmp("qpT", 64, [P, SETS, T])
        scores1 = tmp("scores1", 64, [P, SETS, NKEYS])
        scores0 = tmp("scores0", 80, [P, SETS, NKEYS])
        top_v = tmp("top_v", RETRIEVED, [P, TB * SETS, TOPK])
        top_i = tmp("top_i", 90, [P, TB * SETS, TOPK])
        fin_v = tmp("fin_v", 92, [P, TB * PH, TOPK])
        fin_i = tmp("fin_i", 93, [P, TB * PH, TOPK], U32)
        a_u = tmp("a_u", 94, [P, TB * PH * TOPK], U32)
        b_u = tmp("b_u", 95, [P, TB * PH * TOPK], U32)
        a_f = tmp("a_f", 96, [P, TB * PH * TOPK])
        b_f = tmp("b_f", 97, [P, TB * PH * TOPK])
        row_f = tmp("row_f", 98, [P, TB * PH * TOPK])
        col_f = tmp("col_f", 99, [P, TB * PH * TOPK])
        g_exp = tmp("g_exp", 100, [P, TB * PH, TOPK])
        g_sum = tmp("g_sum", 101, [P, TB * PH])
        pick = tmp("pick", 104, [P, TB * PH * TOPK, TOPK])
        top_u = tmp("top_u", 104, [P, TB * SETS, TOPK], U32)
        cand = tmp("cand", 106, [P, 2, TOPK * TOPK])
        struck = tmp("struck", 108, [P, 2, TOPK * TOPK])

        ps = ctx.enter_context(nc.psum_tensor("ps", [P, 8, 512], FP32))

        def pair(b0, n):
            return ps[:, b0:b0 + n // 2, :].rearrange("p b (i t) -> p (b i) t", i=2)

        def sem(name):
            return ctx.enter_context(nc.semaphore(name))

        raw_loaded = [sem(f"raw_loaded{j}") for j in range(RING)]
        hi_ready, lo_ready, slab_done = sem("hi_ready"), sem("lo_ready"), sem("slab_done")
        act_evac, dve_evac = sem("act_evac"), sem("dve_evac")
        x_loaded, x_ffn, par_loaded = sem("x_loaded"), sem("x_ffn"), sem("par_loaded")
        mem_loaded, keys_loaded, out_stored = sem("mem_loaded"), sem("keys_loaded"), sem("out_stored")
        consts, const_step, pool_step = sem("consts"), sem("const_step"), sem("pool_step")
        sq_ready, ms_ready, xn_ready = sem("sq_ready"), sem("ms_ready"), sem("xn_ready")
        root_ready, hroot_ready, abs_ready = sem("root_ready"), sem("hroot_ready"), sem("abs_ready")
        act_hi_ready, act_ready = sem("act_hi_ready"), sem("act_ready")
        wif_hi_ready, wif_ready, gates_mm = sem("wif_hi_ready"), sem("wif_ready"), sem("gates_mm")
        nf_ready, lnf_ready, ls_ready = sem("nf_ready"), sem("lnf_ready"), sem("ls_ready")
        cum_ready, r_ready, rows_mm = sem("cum_ready"), sem("r_ready"), sem("rows_mm")
        eb_ready, e_ready, bc_mm = sem("eb_ready"), sem("e_ready"), sem("bc_mm")
        v_tr, v_nat_ready, vmem_tr, vmem_ready = sem("v_tr"), sem("v_nat_ready"), sem("vmem_tr"), sem("vmem_ready")
        o_ready, qk_mm, arg_ready, dw_ready = sem("o_ready"), sem("qk_mm"), sem("arg_ready"), sem("dw_ready")
        s_ready, nd_mm, hl_ready, hsq_ready, hms_mm = (sem("s_ready"), sem("nd_mm"), sem("hl_ready"),
                                                      sem("hsq_ready"), sem("hms_mm"))
        xs_mm, nmax_ready, exp_ready, prob_ready = sem("xs_mm"), sem("nmax_ready"), sem("exp_ready"), sem("prob_ready")
        pt_mm, pt_dve, pt_act, xo_mm = sem("pt_mm"), sem("pt_dve"), sem("pt_act"), sem("xo_mm")
        sc_mm, sc_evac, fin_ready, gexp_ready = sem("sc_mm"), sem("sc_evac"), sem("fin_ready"), sem("gexp_ready")
        keys_read, decoded, ret_mm, cols_ready = sem("keys_read"), sem("decoded"), sem("ret_mm"), sem("cols_ready")
        hot_act_ready, y_ready, y_act_ready, y_mm = sem("hot_act_ready"), sem("y_ready"), sem("y_act_ready"), sem("y_mm")
        hot_col_ready, hot_row_ready, gate_mm = sem("hot_col_ready"), sem("hot_row_ready"), sem("gate_mm")
        gated_ready, ga_hi_ready, ga_ready = sem("gated_ready"), sem("ga_hi_ready"), sem("ga_ready")
        settled = sem("settled")
        act_step, dve_step, out_ready = sem("act_step"), sem("dve_step"), sem("out_ready")

        def settle(eng):
            eng.sem_inc(settled, 1)

        block = ctx.enter_context(nc.Block())

        @block.sync
        def _(sp):
            def load(j, slab):
                sp.dma_start(raw[:, j, :], slab).then_inc(raw_loaded[j], 16)

            sp.dma_start(xT[:], x).then_inc(x_loaded, 16)
            sp.dma_start(gfin[:], g_final).then_inc(x_loaded, 16)
            for j in range(RING):
                load(j, slabs[j])
            with sp.Fori(1, DEPTH * SLABS // RING) as g:
                for j in range(RING):
                    sp.wait_ge(lo_ready, g * RING + (j - RING + 1))
                    load(j, slabs[ds(g * RING + j, 1)].rearrange("o p f -> (o p) f"))
            for j in range(RING):
                sp.wait_ge(lo_ready, DEPTH * SLABS - RING + j + 1)
                load(j, slabs[j])
            sp.wait_ge(out_ready, 1)
            sp.dma_start(out, xn[:]).then_inc(out_stored, 16)
            sp.wait_ge(out_stored, 16)

        @block.gpsimd
        def _(pool):
            nc.gpsimd.memset(ident[:], 0.0).then_inc(const_step, 1)
            nc.gpsimd.memset(ones[:], 1.0).then_inc(const_step, 1)
            nc.gpsimd.memset(eps[:], EPS).then_inc(consts, 1)
            pool.wait_ge(const_step, 2)
            nc.gpsimd.affine_select(out=ident[:], in_=ident[:], compare_op=ALU.not_equal, fill=1.0,
                                    base=0, pattern=[[-1, P]], channel_multiplier=1).then_inc(consts, 1)
            nc.gpsimd.affine_select(out=tri[:], in_=ones[:], compare_op=ALU.is_ge, fill=0.0,
                                    base=0, pattern=[[1, P]], channel_multiplier=-1).then_inc(consts, 1)
            nc.gpsimd.iota(iota[:], [[1, P]], base=0, channel_multiplier=0,
                           allow_small_or_imprecise_dtypes=True).then_inc(consts, 1)
            with pool.Fori(0, DEPTH) as layer:
                pool.wait_ge(x_ffn, layer + 1)
                pool.dma_start(par[:], params[ds(layer, 1)].rearrange("o p f -> (o p) f")).then_inc(par_loaded, 16)
                pool.dma_start(memT[:], mem).then_inc(mem_loaded, 16)
                pool.dma_start(skT[:], sub_keys[ds(layer, 1)].rearrange("o p s k -> (o p) s k")).then_inc(keys_loaded, 16)
                pool.wait_ge(cols_ready, layer + 1)
                pool.wait_ge(slab_done, layer * SLABS + V_AT)
                settle(pool)
                with pool.Fori(0, GROUPS // RING) as g:
                    nc.gpsimd.tensor_copy(cols16[:], colT[:, ds(g * (4 * RING), 4 * RING)]).then_inc(pool_step, 1)
                    pool.wait_ge(pool_step, layer * (GROUPS // RING) + g + 1)
                    for s in range(RING):
                        pool.wait_ge(gate_mm, layer * GROUPS + g * RING + s + 1)
                        settle(pool)
                        for i in range(POOL_TOKENS[s]):
                            last = nc.gpsimd.tensor_scalar(hot_col[:, s, i, :], iota[:],
                                                           cols16[:, 4 * s + i:4 * s + i + 1], None, ALU.is_equal)
                        last.then_inc(hot_col_ready, 1)
                    pool.wait_ge(hot_col_ready, layer * GROUPS + g * RING + RING)

        @block.scalar
        def _(act):
            step = Steps(act, act_step)

            def turn(layer, at0, g, evac):
                for j in range(RING):
                    n = layer * SLABS + at0 + g * RING + j
                    act.wait_ge(slab_done, n + 1)
                    if evac is not None:
                        evac(j, g * RING + j).then_inc(act_evac, 1)
                    hi_part_next(j, layer, at0, g)

            def hi_part_next(j, layer, at0, g):
                act.wait_ge(raw_loaded[j], (layer * (SLABS // RING) + (at0 // RING + 2) + g) * 16)
                nc.scalar.activation(w_hi[:, j].rearrange("p k c -> p (k c)"), raw[:, j, :],
                                     ACT.Copy).then_inc(hi_ready, 1)

            def section(layer, at0, slabs_n, evac=None):
                with act.Fori(0, slabs_n // RING) as g:
                    turn(layer, at0, g, evac)

            def copy_to(dst):
                return lambda j, n: nc.scalar.activation(dst[:, ds(n, 1), :], ps[:, j:j + 1, 0:T], ACT.Copy)

            def squares(src, layer, norm):
                nc.scalar.activation(sq[:], src[:], ACT.Square, scale=D ** -0.5).then_inc(sq_ready, 1)
                act.wait_ge(ms_ready, norm + 1 if layer is None else layer * NORMS + norm + 1)
                nc.scalar.activation(rstd[:], ps[:, 7, 0:T], ACT.Sqrt, bias=eps[:]).then_inc(root_ready, 1)

            def operand_hi(layer, use, free_at=None):
                if free_at is not None:
                    act.wait_ge(slab_done, layer * SLABS + free_at)
                for half in range(2):
                    act.wait_ge(xn_ready, layer * (2 * USES) + 2 * use + half + 1)
                    nc.scalar.activation(act_hi[:, 4 * half:4 * half + 4], xn[:, 4 * half:4 * half + 4],
                                         ACT.Copy).then_inc(act_hi_ready, 1)

            act.wait_ge(consts, 4)
            nc.scalar.sem_inc(act_evac, RING)
            for j in range(RING):
                act.wait_ge(raw_loaded[j], 16)
                nc.scalar.activation(w_hi[:, j].rearrange("p k c -> p (k c)"), raw[:, j, :],
                                     ACT.Copy).then_inc(hi_ready, 1)
            with act.Fori(0, DEPTH) as layer:
                act.wait_ge(x_ffn, layer + 1)
                squares(xT, layer, NORM_MIX)
                act.wait_ge(par_loaded, layer * 16 + 16)
                nc.scalar.activation(wif_hi[:].rearrange("p k c -> p (k c)"), par[:, W_IF:W_IF + KB * 8],
                                     ACT.Copy).then_inc(wif_hi_ready, 1)
                operand_hi(layer, USE_MIX)
                section(layer, IN_AT, IN_SLABS, copy_to(zT))
                act.wait_ge(mem_loaded, layer * 16 + 16)
                squares(memT, layer, NORM_MEM)
                act.wait_ge(gates_mm, layer + 1)
                operand_hi(layer, USE_MEM, KV_AT)
                act.wait_ge(nf_ready, layer + 1)
                step.link(nc.scalar.activation(ef[:], nf[:], ACT.Exp))
                nc.scalar.activation(ef[:], ef[:], ACT.Ln, bias=1.0).then_inc(lnf_ready, 1)
                step.restart()
                nc.scalar.activation(o_sig[:], zT[:, 24:28, :], ACT.Sigmoid).then_inc(o_ready, 1)
                section(layer, KV_AT, KV_SLABS, copy_to(kvT))
                act.wait_ge(v_tr, layer + 1)
                nc.scalar.activation(v_nat[:].rearrange("p b h c -> p (b h c)"),
                                     ps[:, 5:7, :].rearrange("p b c -> p (b c)"), ACT.Copy).then_inc(v_nat_ready, 1)
                act.wait_ge(vmem_tr, layer + 1)
                nc.scalar.activation(v_mem[:].rearrange("p b c -> p (b c)"),
                                     ps[:, 0:4, :].rearrange("p b c -> p (b c)"), ACT.Copy).then_inc(vmem_ready, 1)
                act.wait_ge(eb_ready, layer + 1)
                nc.scalar.activation(e_row[:], e_row[:], ACT.Exp, scale=-1.0).then_inc(e_ready, 1)
                act.wait_ge(arg_ready, layer + 1)
                nc.scalar.activation(arg[:], arg[:], ACT.Exp, scale=-1.0).then_inc(dw_ready, 1)
                act.wait_ge(nd_mm, layer + 1)
                nc.scalar.activation(den[:], pair(4, 4), ACT.Abs).then_inc(abs_ready, 1)
                act.wait_ge(hl_ready, layer + 1)
                nc.scalar.activation(den[:], hl[:], ACT.Square).then_inc(hsq_ready, 1)
                act.wait_ge(hms_mm, layer + 1)
                nc.scalar.activation(o_sig[:], pair(6, 4), ACT.Sqrt, bias=eps[:], scale=1.0 / P).then_inc(hroot_ready, 1)
                operand_hi(layer, USE_Y, OUT_AT)
                section(layer, OUT_AT, OUT_SLABS)
                act.wait_ge(dve_evac, layer * DVE_EVS + OUT_SLABS + RING)
                squares(xT, layer, NORM_XATTN)
                operand_hi(layer, USE_XATTN, Q_AT)
                section(layer, Q_AT, Q_SLABS, copy_to(qT))
                act.wait_ge(nmax_ready, layer + 1)
                for i in range(2 * XH):
                    last = nc.scalar.activation(prob[:, i, :], pair(4, 8)[:, i, :], ACT.Exp, bias=nmax[:, i:i + 1],
                                                scale=X_SCALE, accum_out=rsum[:, i:i + 1])
                last.then_inc(exp_ready, 1)
                act.wait_ge(pt_mm, layer + 1)
                nc.scalar.activation(probT[:, 1], pair(2, 4), ACT.Copy).then_inc(pt_act, 1)
                operand_hi(layer, USE_AO, XO_AT)
                section(layer, XO_AT, XO_SLABS)
                act.wait_ge(dve_evac, (layer + 1) * DVE_EVS + RING)
                squares(xT, layer, NORM_FFN)
                operand_hi(layer, USE_FFN, PQ_AT)
                section(layer, PQ_AT, PQ_SLABS, copy_to(qpT))

                def gelu_to(first):
                    return lambda j, n: nc.scalar.activation(gated[:, ds(n + first, 1), :], ps[:, j:j + 1, 0:T], ACT.Gelu)

                def scores_out(b, dst):
                    act.wait_ge(sc_mm, layer * TB + b + 1)
                    nc.scalar.activation(dst[:].rearrange("p n k -> p (n k)"),
                                         ps[:, 4:8, :].rearrange("p b c -> p (b c)"), ACT.Copy).then_inc(sc_evac, 1)

                scores_out(0, scores0)
                section(layer, U_AT, RING, gelu_to(0))
                scores_out(1, scores1)
                section(layer, U_AT + RING, KEYS_READ - RING, gelu_to(RING))
                act.wait_ge(keys_read, layer + 1)
                section(layer, U_AT + KEYS_READ, RING, gelu_to(KEYS_READ))
                act.wait_ge(fin_ready, layer + 1)
                nc.scalar.activation(g_exp[:], g_exp[:], ACT.Exp).then_inc(gexp_ready, 1)
                section(layer, U_AT + KEYS_READ + RING, RETRIEVED - KEYS_READ - RING, gelu_to(KEYS_READ + RING))
                act.wait_ge(ret_mm, layer + 1)
                section(layer, U_AT + RETRIEVED, U_SLABS - RETRIEVED, gelu_to(RETRIEVED))

                def gated_hi(j, n):
                    nc.scalar.activation(act_hi[:, j:j + 1, :], gated[:, n, :], ACT.Copy).then_inc(ga_hi_ready, 1)

                act.wait_ge(cols_ready, layer + 1)
                settle(act)
                with act.Fori(0, GROUPS // RING) as g:
                    for s in range(RING):
                        first = POOL_TOKENS[s]
                        act.wait_ge(gate_mm, layer * GROUPS + g * RING + s + 1)
                        settle(act)
                        for i in range(first, 4):
                            last = nc.scalar.activation(hot_col[:, s, i, :], iota[:], ACT.Abs, scale=-1.0,
                                                        bias=colT[:, ds(g * (4 * RING) + 4 * s + i, 1)])
                        step.mark(last)
                        if s % 2 == 1:
                            step.join()
                            for q in (s - 1, s):
                                first = POOL_TOKENS[q]
                                nc.scalar.activation(hot_col[:, q, first:4, :], hot_col[:, q, first:4, :], ACT.Relu,
                                                     scale=-1.0, bias=ones[:, 0:1]).then_inc(hot_act_ready, 1)
                    step.restart()
                act.wait_ge(gated_ready, layer + 1)
                for j in range(RING):
                    gated_hi(j, slice(j, j + 1))
                with act.Fori(0, V_SLABS // RING - 1) as g:
                    for j in range(RING):
                        act.wait_ge(slab_done, layer * SLABS + V_AT + g * RING + j + 1)
                        hi_part_next(j, layer, V_AT, g)
                        gated_hi(j, ds(g * RING + RING + j, 1))
                for j in range(RING):
                    act.wait_ge(slab_done, layer * SLABS + SLABS - RING + j + 1)
                    act.wait_ge(raw_loaded[j], (layer + 1) * (SLABS // RING * 16) + 16)
                    nc.scalar.activation(w_hi[:, j].rearrange("p k c -> p (k c)"), raw[:, j, :],
                                         ACT.Copy).then_inc(hi_ready, 1)
                act.wait_ge(slab_done, layer * SLABS + SLABS)
                for i in range(2, 4):
                    nc.scalar.activation(y_nat[:, i, :], ps[:, i, :], ACT.Copy).then_inc(y_act_ready, 1)
            act.wait_ge(x_ffn, DEPTH + 1)
            squares(xT, None, DEPTH * NORMS)

        @block.vector
        def _(dve):
            step = Steps(dve, dve_step)

            def lo_part(layer, at0, g, j):
                dve.wait_ge(hi_ready, layer * SLABS + at0 + g * RING + j + 1)
                nc.vector.tensor_tensor(w_lo[:, j].rearrange("p k c -> p (k c)"), raw[:, j, :],
                                        w_hi[:, j].rearrange("p k c -> p (k c)").bitcast(FP32),
                                        ALU.subtract).then_inc(lo_ready, 1)

            def section(layer, at0, slabs_n, evac=None):
                with dve.Fori(0, slabs_n // RING) as g:
                    for j in range(RING):
                        if evac is not None:
                            dve.wait_ge(slab_done, layer * SLABS + at0 + g * RING + j + 1)
                            evac(j, g * RING + j).then_inc(dve_evac, 1)
                        lo_part(layer, at0 + RING, g, j)

            def add_to_x(j, n):
                return nc.vector.tensor_tensor(xT[:, ds(n, 1), :], xT[:, ds(n, 1), :], ps[:, j:j + 1, 0:T], ALU.add)

            def norm(src, g_col, norm_count, half_done):
                dve.wait_ge(root_ready, norm_count)
                step.link(nc.vector.reciprocal(rstd[:], rstd[:]))
                for half in range(2):
                    for k in range(4 * half, 4 * half + 4):
                        last = nc.vector.scalar_tensor_tensor(xn[:, k, :], src[:, k, :], g_col[:, k:k + 1], rstd[:],
                                                              ALU.mult, ALU.mult)
                    half_done(last)

            def operand_lo(layer, use):
                for half in range(2):
                    h = slice(4 * half, 4 * half + 4)
                    dve.wait_ge(act_hi_ready, layer * (2 * USES) + 2 * use + half + 1)
                    nc.vector.tensor_tensor(act_lo[:, h], xn[:, h], act_hi[:, h].bitcast(FP32),
                                            ALU.subtract).then_inc(act_ready, 1)

            def to_xn(ins):
                ins.then_inc(xn_ready, 1)

            nc.vector.sem_inc(dve_evac, RING)
            dve.wait_ge(x_loaded, 32)
            nc.vector.sem_inc(x_ffn, 1)
            for j in range(RING):
                dve.wait_ge(hi_ready, j + 1)
                nc.vector.tensor_tensor(w_lo[:, j].rearrange("p k c -> p (k c)"), raw[:, j, :],
                                        w_hi[:, j].rearrange("p k c -> p (k c)").bitcast(FP32),
                                        ALU.subtract).then_inc(lo_ready, 1)
            dve.wait_ge(consts, 4)
            with dve.Fori(0, DEPTH) as layer:
                dve.wait_ge(wif_hi_ready, layer + 1)
                nc.vector.tensor_tensor(wif_lo[:].rearrange("p k c -> p (k c)"), par[:, W_IF:W_IF + KB * 8],
                                        wif_hi[:].rearrange("p k c -> p (k c)").bitcast(FP32),
                                        ALU.subtract).then_inc(wif_ready, 1)
                norm(xT, par[:, G_MIX:G_MIX + 8], layer * NORMS + NORM_MIX + 1, to_xn)
                operand_lo(layer, USE_MIX)
                section(layer, IN_AT, IN_SLABS)
                norm(memT, par[:, G_MEM:G_MEM + 8], layer * NORMS + NORM_MEM + 1, to_xn)
                operand_lo(layer, USE_MEM)
                dve.wait_ge(gates_mm, layer + 1)
                step.link(nc.vector.tensor_tensor(
                    gates[:], ps[:, 4, 0:16].rearrange("p (b c) -> p b c", b=TB),
                    par[:, B_IF:B_IF + 8].unsqueeze(1).to_broadcast([P, TB, 8]), ALU.add))
                nc.vector.scalar_tensor_tensor(nf[:], gates[:, :, 4:8], -1.0, gates[:, :, 4:8], ALU.mult, ALU.min).then_inc(nf_ready, 1)
                step.mark(nc.vector.tensor_scalar(mf[:], gates[:, :, 4:8], 0.0, None, ALU.min))
                section(layer, KV_AT, KV_SLABS)
                dve.wait_ge(lnf_ready, layer + 1)
                step.join()
                nc.vector.tensor_tensor(ls[:], mf[:], ef[:], ALU.subtract).then_inc(ls_ready, 1)
                nc.vector.memset(u_pad[:, :, 0:2], 0.0)
                dve.wait_ge(act_evac, layer * ACT_EVS + KV_EV + RING)
                step.link(nc.vector.tensor_tensor(u_pad[:, :, 2:T + 2], zT[:, 8:12, :], zT[:, 0:4, :], ALU.mult))
                for m in range(4):
                    last = nc.vector.tensor_scalar(conv[:, m, :], u_pad[:, m, 2:T + 2],
                                                   par[:, CONV_W + 8 + m:CONV_W + 9 + m], par[:, CONV_B + m:CONV_B + m + 1],
                                                   ALU.mult, ALU.add)
                step.link(last)
                for tap in (1, 0):
                    for m in range(4):
                        last = nc.vector.scalar_tensor_tensor(conv[:, m, :], u_pad[:, m, tap:tap + T],
                                                              par[:, CONV_W + 4 * tap + m:CONV_W + 4 * tap + m + 1],
                                                              conv[:, m, :], ALU.mult, ALU.add)
                    step.link(last)
                nc.vector.tensor_tensor(xn[:, 0:4, :], conv[:], zT[:, 4:8, :], ALU.mult).then_inc(xn_ready, 1)
                dve.wait_ge(cum_ready, layer + 1)
                step.link(nc.vector.tensor_copy(b_nat[:], ps[:, 7, 0:8].rearrange("p (b h) -> p b h", b=TB)))
                nc.vector.tensor_tensor(r_nat[:], gates[:, :, 0:4], b_nat[:], ALU.subtract).then_inc(r_ready, 1)
                dve.wait_ge(rows_mm, layer + 1)
                step.link(nc.vector.tensor_copy(r_row[:], ps[0:4, 7, 0:T]))
                step.link(nc.vector.tensor_tensor_scan(m_row[:], r_row[:], r_row[:], 0.0, ALU.max, ALU.max))
                nc.vector.tensor_tensor(e_row[:], m_row[:], ps[0:4, 7, T:2 * T], ALU.add).then_inc(eb_ready, 1)
                dve.wait_ge(bc_mm, layer + 1)
                for h in range(LH):
                    m_bc = pair(0, 4)[:, h, :]
                    nc.vector.tensor_scalar(arg[:, h, 0:T], m_bc, r_nat[:, 0, h:h + 1], 0.0, ALU.subtract, ALU.max)
                    last = nc.vector.tensor_scalar(arg[:, h, T:384], m_bc[:, P:T], r_nat[:, 1, h:h + 1], 0.0,
                                                   ALU.subtract, ALU.max)
                last.then_inc(arg_ready, 1)
                dve.wait_ge(dw_ready, layer + 1)
                diag = arg[:].rearrange("p h (i t) -> p h i t", i=3)[:, :, 0:3:2, :]
                step.link(nc.vector.tensor_tensor(diag, diag, tri[:].unsqueeze(1).unsqueeze(1).to_broadcast([P, LH, 2, P]),
                                                  ALU.mult))
                dve.wait_ge(qk_mm, layer + 1)
                for h in range(LH):
                    last = nc.vector.scalar_tensor_tensor(s_w[:, h, :], ps[:, 4 + h, 0:384], LSTM_SCALE, arg[:, h, :],
                                                          ALU.mult, ALU.mult)
                last.then_inc(s_ready, 1)
                dve.wait_ge(abs_ready, layer + 1)
                step.link(nc.vector.tensor_tensor(den[:], den[:], pair(2, 4), ALU.max))
                step.link(nc.vector.reciprocal(den[:], den[:]))
                step.link(nc.vector.tensor_tensor(hl[:], pair(0, 4), den[:], ALU.mult))
                dve.wait_ge(o_ready, layer + 1)
                nc.vector.tensor_tensor(hl[:], hl[:], o_sig[:], ALU.mult).then_inc(hl_ready, 1)
                dve.wait_ge(hroot_ready, layer + 1)
                step.link(nc.vector.reciprocal(o_sig[:], o_sig[:]))
                for h in range(LH):
                    last = nc.vector.scalar_tensor_tensor(xn[:, 4 + h, :], hl[:, h, :], par[:, G_HEAD + h:G_HEAD + h + 1],
                                                          o_sig[:, h, :], ALU.mult, ALU.mult)
                last.then_inc(xn_ready, 1)
                operand_lo(layer, USE_Y)
                section(layer, OUT_AT, OUT_SLABS, add_to_x)
                dve.wait_ge(dve_evac, layer * DVE_EVS + OUT_SLABS + RING)
                norm(xT, par[:, G_XATTN:G_XATTN + 8], layer * NORMS + NORM_XATTN + 1, to_xn)
                operand_lo(layer, USE_XATTN)
                section(layer, Q_AT, Q_SLABS)
                dve.wait_ge(xs_mm, layer + 1)
                step.link(nc.vector.tensor_reduce(rmax[:], pair(4, 8), AX.X, ALU.max))
                nc.vector.tensor_scalar(nmax[:], rmax[:], -X_SCALE, None, ALU.mult).then_inc(nmax_ready, 1)
                dve.wait_ge(exp_ready, layer + 1)
                step.link(nc.vector.reciprocal(rinv[:], rsum[:]))
                nc.vector.tensor_tensor(prob[:], prob[:], rinv[:].unsqueeze(2).to_broadcast([P, 2 * XH, NMEM]),
                                        ALU.mult).then_inc(prob_ready, 1)
                dve.wait_ge(pt_mm, layer + 1)
                nc.vector.tensor_copy(probT[:, 0], pair(0, 4)).then_inc(pt_dve, 1)
                dve.wait_ge(xo_mm, layer + 1)
                for half in range(2):
                    nc.vector.tensor_copy(xn[:, 4 * half:4 * half + 4, :], pair(4 + 2 * half, 4)).then_inc(xn_ready, 1)
                operand_lo(layer, USE_AO)
                section(layer, XO_AT, XO_SLABS, add_to_x)
                dve.wait_ge(dve_evac, (layer + 1) * DVE_EVS + RING)
                norm(xT, par[:, G_FFN:G_FFN + 8], layer * NORMS + NORM_FFN + 1, to_xn)
                operand_lo(layer, USE_FFN)
                section(layer, PQ_AT, PQ_SLABS)

                def slab(i):
                    lo_part(layer, U_AT + i - i % RING, 0, i % RING)

                def top16(first, second, beside):
                    rows = (first, second)
                    for src, _, v, _ in rows:
                        step.mark(nc.vector.max(v[:, 0:8], src))
                    slab(beside)
                    step.join()
                    for src, struck, v, i in rows:
                        nc.vector.max_index(i[:, 0:8], v[:, 0:8], src)
                        step.mark(nc.vector.match_replace(struck, v[:, 0:8], src, LOWEST))
                    slab(beside + 1)
                    step.join()
                    for _, struck, v, _ in rows:
                        step.mark(nc.vector.max(v[:, 8:16], struck))
                    step.join()
                    for _, struck, v, i in rows:
                        step.mark(nc.vector.max_index(i[:, 8:16], v[:, 8:16], struck))

                for n in range(0, TB * SETS, 2):
                    if n % SETS == 0:
                        dve.wait_ge(sc_evac, layer * TB + n // SETS + 1)
                        settle(dve)
                    src = (scores0, scores1)[n // SETS]
                    step.join()
                    top16(*[(src[:, m % SETS, :], struck[:, m - n, 0:NKEYS], top_v[:, m, :], top_u[:, m, :])
                            for m in (n, n + 1)], beside=n + RING)
                step.join()
                nc.vector.tensor_copy(top_i[:], top_u[:]).then_inc(keys_read, 1)
                for n in range(0, TB * PH, 2):
                    step.join()
                    for m in (n, n + 1):
                        step.mark(nc.vector.tensor_tensor(
                            cand[:, m - n, :].rearrange("p (a b) -> p a b", a=TOPK),
                            top_v[:, 2 * m, :].unsqueeze(2).to_broadcast([P, TOPK, TOPK]),
                            top_v[:, 2 * m + 1, :].unsqueeze(1).to_broadcast([P, TOPK, TOPK]), ALU.add))
                    slab(RING + TB * SETS + 2 * n)
                    step.join()
                    top16(*[(cand[:, m - n, :], struck[:, m - n, :], fin_v[:, m, :], fin_i[:, m, :])
                            for m in (n, n + 1)], beside=RING + TB * SETS + 2 * n + 1)
                    slab(RING + TB * SETS + 2 * n + 3)
                step.join()
                at_slab = RING + TB * SETS + 2 * TB * PH
                nc.vector.tensor_tensor(g_exp[:], fin_v[:], fin_v[:, :, 0:1].to_broadcast([P, TB * PH, TOPK]),
                                        ALU.subtract).then_inc(fin_ready, 1)
                flat_i = fin_i[:].rearrange("p c k -> p (c k)")
                step.mark(nc.vector.tensor_scalar(a_u[:], flat_i, 4, None, ALU.logical_shift_right))
                step.mark(nc.vector.tensor_scalar(b_u[:], flat_i, 15, None, ALU.bitwise_and))
                slab(at_slab)
                step.join()
                step.mark(nc.vector.tensor_copy(a_f[:], a_u[:]))
                step.mark(nc.vector.tensor_copy(b_f[:], b_u[:]))
                slab(at_slab + 1)
                keys = top_i[:].rearrange("p (c s) a -> p c s a", s=2)
                pick4 = pick[:].rearrange("p (c k) a -> p c k a", k=TOPK)
                n = at_slab + 2
                for side, (place, found) in enumerate(((a_f, row_f), (b_f, col_f))):
                    step.join()
                    step.mark(nc.vector.tensor_tensor(
                        pick[:], place[:].unsqueeze(2).to_broadcast([P, TB * PH * TOPK, TOPK]),
                        iota[:, 0:TOPK].unsqueeze(1).to_broadcast([P, TB * PH * TOPK, TOPK]), ALU.is_equal))
                    for i in range(3):
                        slab(n + i)
                    step.join()
                    step.mark(nc.vector.tensor_tensor(
                        pick4, pick4, keys[:, :, side, :].unsqueeze(2).to_broadcast([P, TB * PH, TOPK, TOPK]), ALU.mult))
                    for i in range(3, 6):
                        slab(n + i)
                    step.join()
                    step.mark(nc.vector.tensor_reduce(found[:], pick[:], AX.X, ALU.add))
                    for i in range(6, 8):
                        slab(n + i)
                    n += 8
                step.join()
                dve.wait_ge(gexp_ready, layer + 1)
                step.mark(nc.vector.tensor_reduce(g_sum[:], g_exp[:], AX.X, ALU.add))
                slab(n)
                step.join()
                step.mark(nc.vector.reciprocal(g_sum[:], g_sum[:]))
                slab(n + 1)
                step.join()
                nc.vector.tensor_tensor(g_exp[:], g_exp[:], g_sum[:].unsqueeze(2).to_broadcast([P, TB * PH, TOPK]),
                                        ALU.mult).then_inc(decoded, 1)
                assert n + 2 == RETRIEVED, n
                section(layer, U_AT + RETRIEVED - RING, RING)
                dve.wait_ge(ret_mm, layer + 1)
                step.mark(nc.vector.tensor_copy(rowT[:], ps[:, 4, 0:T]))
                step.mark(nc.vector.tensor_copy(gateT[:], ps[:, 5, 0:T]))
                nc.vector.tensor_copy(colT[:], ps[:, 4, T:2 * T]).then_inc(cols_ready, 1)
                section(layer, U_AT + RETRIEVED, U_SLABS - RETRIEVED)
                step.join()

                def hot(n, s):
                    dve.wait_ge(gate_mm, layer * GROUPS + n + 1)
                    for i in range(4):
                        t = n * 4 + i
                        last = nc.vector.tensor_scalar(hot_row[:, s, i, :], iota[:], rowT[:, ds(t, 1)],
                                                       gateT[:, ds(t, 1)], ALU.is_equal, ALU.mult)
                    last.then_inc(hot_row_ready, 1)

                def gate(n, s, final=False):
                    dve.wait_ge(gate_mm, layer * GROUPS + n + 1 + RING)
                    g4 = gated[:, :, ds(n * 4, 4)].rearrange("p i t -> p t i")
                    return nc.vector.tensor_tensor(g4, g4, ps[:, 4 + s, :].rearrange("p (t i) -> p t i", t=4), ALU.mult)

                dve.wait_ge(slab_done, layer * SLABS + V_AT)
                hot(0, 0)
                hot(1, 1)
                dve.wait_ge(act_evac, (layer + 1) * ACT_EVS + RING)
                settle(dve)
                with dve.Fori(0, GROUPS // RING - 1) as g:
                    for s in range(RING):
                        hot(g * RING + s + 2, (s + 2) % RING)
                        gate(g * RING + s, s)
                hot(GROUPS - 2, 2)
                gate(GROUPS - 4, 0)
                hot(GROUPS - 1, 3)
                for s in (1, 2, 3):
                    last = gate(GROUPS - 4 + s, s)
                last.then_inc(gated_ready, 1)

                def gated_lo(j, n, ready):
                    dve.wait_ge(ga_hi_ready, ready)
                    nc.vector.tensor_tensor(act_lo[:, j:j + 1, :], gated[:, n, :], act_hi[:, j:j + 1, :].bitcast(FP32),
                                            ALU.subtract).then_inc(ga_ready, 1)

                for j in range(RING):
                    gated_lo(j, slice(j, j + 1), layer * V_SLABS + j + 1)
                with dve.Fori(0, V_SLABS // RING - 1) as g:
                    for j in range(RING):
                        lo_part(layer, V_AT + RING, g, j)
                        gated_lo(j, ds(g * RING + RING + j, 1), layer * V_SLABS + g * RING + RING + j + 1)
                for j in range(RING):
                    lo_part(layer, SLABS, 0, j)
                dve.wait_ge(slab_done, layer * SLABS + SLABS)
                for i in range(2):
                    nc.vector.tensor_copy(y_nat[:, i, :], ps[:, i, :]).then_inc(y_ready, 1)
                dve.wait_ge(y_mm, layer + 1)
                for m in range(4):
                    last = nc.vector.tensor_tensor(xT[:, 2 * m:2 * m + 2, :], xT[:, 2 * m:2 * m + 2, :],
                                                   pair(4, 8)[:, 2 * m:2 * m + 2, :], ALU.add)
                last.then_inc(x_ffn, 1)
                step.restart()
            dve.wait_ge(x_ffn, DEPTH + 1)
            norm(xT, gfin[:], DEPTH * NORMS + 1, step.mark)
            step.join()
            nc.vector.sem_inc(out_ready, 1)

        @block.tensor
        def _(pe):
            PARTS = ((w_hi, act_hi), (w_lo, act_hi), (w_hi, act_lo))

            def project(layer, at0, slabs_n, evac, ev_at, ev_per_layer):
                settle(pe)
                with pe.Fori(0, slabs_n // RING) as g:
                    for j in range(RING):
                        pe.wait_ge(lo_ready, layer * SLABS + at0 + g * RING + j + 1)
                        pe.wait_ge(evac, layer * ev_per_layer + ev_at + g * RING + j + 1)
                        for k in range(KB):
                            for i, (w, a) in enumerate(PARTS):
                                last = nc.tensor.matmul(ps[:, j, 0:T], w[:, j, k, :], a[:, k, :],
                                                        start=(k == 0 and i == 0), stop=(k == KB - 1 and i == 2))
                        last.then_inc(slab_done, 1)

            def mean_square(count):
                pe.wait_ge(sq_ready, count)
                for k in range(KB):
                    last = nc.tensor.matmul(ps[:, 7, 0:T], ones[:], sq[:, k, :], start=(k == 0), stop=(k == KB - 1))
                last.then_inc(ms_ready, 1)

            def operand(layer, use):
                pe.wait_ge(act_ready, layer * (2 * USES) + 2 * use + 2)

            nc.tensor.sem_inc(gate_mm, RING)
            pe.wait_ge(consts, 4)
            with pe.Fori(0, DEPTH) as layer:
                mean_square(layer * NORMS + NORM_MIX + 1)
                operand(layer, USE_MIX)
                project(layer, IN_AT, IN_SLABS, act_evac, IN_EV, ACT_EVS)
                pe.wait_ge(wif_ready, layer + 1)
                for b in range(TB):
                    for k in range(KB):
                        for i, (a, w) in enumerate(((act_hi, wif_hi), (act_lo, wif_hi), (act_hi, wif_lo))):
                            last = nc.tensor.matmul(ps[:, 4, 8 * b:8 * b + 8], a[:, k, b * P:(b + 1) * P], w[:, k, :],
                                                    start=(k == 0 and i == 0), stop=(k == KB - 1 and i == 2))
                last.then_inc(gates_mm, 1)
                mean_square(layer * NORMS + NORM_MEM + 1)
                operand(layer, USE_MEM)
                project(layer, KV_AT, KV_SLABS, act_evac, KV_EV, ACT_EVS)
                for b in range(TB):
                    for h in range(LH):
                        last = nc.tensor.transpose(ps[:, 5 + b, h * P:(h + 1) * P], zT[:, 20 + h, b * P:(b + 1) * P], ident[:])
                last.then_inc(v_tr, 1)
                pe.wait_ge(act_evac, layer * ACT_EVS + Q_EV + RING)
                for b in range(2):
                    for c in range(KB):
                        last = nc.tensor.transpose(ps[:, 2 * b + c // 4, (c % 4) * P:(c % 4 + 1) * P],
                                                   kvT[:, 8 + c, b * P:(b + 1) * P], ident[:])
                last.then_inc(vmem_tr, 1)
                pe.wait_ge(ls_ready, layer + 1)
                nc.tensor.matmul(ps[:, 7, 0:4], tri[:], ls[:, 0, :], start=True, stop=True)
                nc.tensor.matmul(ps[:, 7, 4:8], tri[:], ls[:, 1, :], start=True, stop=False)
                nc.tensor.matmul(ps[:, 7, 4:8], ones[:], ls[:, 0, :], start=False, stop=True).then_inc(cum_ready, 1)
                pe.wait_ge(r_ready, layer + 1)
                for i, src in enumerate((r_nat, b_nat)):
                    for b in range(TB):
                        last = nc.tensor.transpose(ps[0:4, 7, i * T + b * P:i * T + (b + 1) * P], src[:, b, :], ident[:])
                last.then_inc(rows_mm, 1)
                pe.wait_ge(vmem_ready, layer + 1)
                pe.wait_ge(e_ready, layer + 1)
                for i, row in enumerate((m_row, e_row)):
                    for h in range(LH):
                        last = nc.tensor.matmul(pair(2 * i, 4)[:, h, :], ident[0:4, h:h + 1].to_broadcast([4, P]), row[:],
                                                start=True, stop=True)
                last.then_inc(bc_mm, 1)
                pe.wait_ge(v_nat_ready, layer + 1)
                for h in range(LH):
                    nc.tensor.matmul(ps[:, 4 + h, 0:T], zT[:, 16 + h, 0:P], zT[:, 12 + h, :], start=True, stop=True)
                    last = nc.tensor.matmul(ps[:, 4 + h, T:384], zT[:, 16 + h, P:T], zT[:, 12 + h, P:T],
                                            start=True, stop=True)
                last.then_inc(qk_mm, 1)
                pe.wait_ge(s_ready, layer + 1)
                for h in range(LH):
                    for bank, lhs in ((0, None), (4, ones)):
                        o = pair(bank, 4)[:, h, :]
                        nc.tensor.matmul(o, v_nat[:, 0, h, :] if lhs is None else lhs[:], s_w[:, h, 0:T],
                                         start=True, stop=False)
                        last = nc.tensor.matmul(o[:, P:T], v_nat[:, 1, h, :] if lhs is None else lhs[:], s_w[:, h, T:384],
                                                start=False, stop=True)
                last.then_inc(nd_mm, 1)
                pe.wait_ge(hsq_ready, layer + 1)
                for i in range(2):
                    last = nc.tensor.matmul(ps[:, 6 + i, :], ones[:], den[:, 2 * i:2 * i + 2, :].rearrange("p i t -> p (i t)"),
                                            start=True, stop=True)
                last.then_inc(hms_mm, 1)
                operand(layer, USE_Y)
                project(layer, OUT_AT, OUT_SLABS, dve_evac, 0, DVE_EVS)
                mean_square(layer * NORMS + NORM_XATTN + 1)
                operand(layer, USE_XATTN)
                project(layer, Q_AT, Q_SLABS, act_evac, Q_EV, ACT_EVS)
                pe.wait_ge(act_evac, layer * ACT_EVS + PQ_EV + RING)
                for b in range(TB):
                    for h in range(XH):
                        for c in range(2):
                            last = nc.tensor.matmul(pair(4, 8)[:, b * XH + h, :], qT[:, 2 * h + c, b * P:(b + 1) * P],
                                                    kvT[:, 2 * h + c, :], start=(c == 0), stop=(c == 1))
                last.then_inc(xs_mm, 1)
                pe.wait_ge(prob_ready, layer + 1)
                for mb in range(2):
                    for h in range(XH):
                        for b in range(TB):
                            last = nc.tensor.transpose(pair(2 * mb, 4)[:, h, b * P:(b + 1) * P],
                                                       prob[:, b * XH + h, mb * P:(mb + 1) * P], ident[:])
                last.then_inc(pt_mm, 1)
                pe.wait_ge(pt_dve, layer + 1)
                pe.wait_ge(pt_act, layer + 1)
                for c in range(KB):
                    for mb in range(2):
                        last = nc.tensor.matmul(pair(4, 8)[:, c, :], v_mem[:, mb, c * P:(c + 1) * P],
                                                probT[:, mb, c // 2, :], start=(mb == 0), stop=(mb == 1))
                last.then_inc(xo_mm, 1)
                operand(layer, USE_AO)
                project(layer, XO_AT, XO_SLABS, dve_evac, OUT_SLABS, DVE_EVS)
                mean_square(layer * NORMS + NORM_FFN + 1)
                operand(layer, USE_FFN)
                project(layer, PQ_AT, PQ_SLABS, act_evac, PQ_EV, ACT_EVS)
                pe.wait_ge(act_evac, layer * ACT_EVS + U_EV + RING)
                pe.wait_ge(keys_loaded, layer * 16 + 16)

                def scores(b):
                    for n in range(SETS):
                        last = nc.tensor.matmul(ps[:, 4 + n // 4, (n % 4) * P:(n % 4 + 1) * P],
                                                qpT[:, n, b * P:(b + 1) * P], skT[:, n, :], start=True, stop=True)
                    last.then_inc(sc_mm, 1)

                scores(0)
                project(layer, U_AT, RING, act_evac, U_EV, ACT_EVS)
                pe.wait_ge(sc_evac, layer * TB + 1)
                scores(1)
                project(layer, U_AT + RING, RETRIEVED - RING, act_evac, U_EV + RING, ACT_EVS)
                pe.wait_ge(decoded, layer + 1)
                for i, src in enumerate((row_f[:], col_f[:], g_exp[:].rearrange("p c k -> p (c k)"))):
                    for b in range(TB):
                        last = nc.tensor.transpose(ps[:, 4 + i // 2, (i % 2) * T + b * P:(i % 2) * T + (b + 1) * P],
                                                   src[:, b * P:(b + 1) * P], ident[:])
                last.then_inc(ret_mm, 1)
                project(layer, U_AT + RETRIEVED, U_SLABS - RETRIEVED, act_evac, U_EV + RETRIEVED, ACT_EVS)

                with pe.Fori(0, GROUPS // RING) as g:
                    for s in range(RING):
                        n = g * RING + s
                        pe.wait_ge(hot_col_ready, layer * GROUPS + n + 1)
                        pe.wait_ge(hot_row_ready, layer * GROUPS + n + 1)
                        pe.wait_ge(hot_act_ready, layer * GROUPS + n + 1)
                        for i in range(4):
                            last = nc.tensor.matmul(ps[:, 4 + s, i * P:(i + 1) * P], hot_col[:, s, i, :],
                                                    hot_row[:, s, i, :], start=True, stop=True)
                        last.then_inc(gate_mm, 1)

                def expert_out(n, j, first=False, final=False):
                    pe.wait_ge(lo_ready, layer * SLABS + V_AT + n + 1)
                    pe.wait_ge(ga_ready, layer * V_SLABS + n + 1)
                    for b in range(TB):
                        for half in range(2):
                            for i, (w, a) in enumerate(PARTS):
                                last = nc.tensor.matmul(ps[:, 2 * b + half, :], a[:, j, b * P:(b + 1) * P],
                                                        w[:, j, 4 * half:4 * half + 4, :].rearrange("p k c -> p (k c)"),
                                                        start=(first and i == 0), stop=(final and i == 2))
                    last.then_inc(slab_done, 1)

                pe.wait_ge(act_evac, (layer + 1) * ACT_EVS + RING)
                for j in range(RING):
                    expert_out(j, j, first=(j == 0))
                with pe.Fori(1, V_SLABS // RING - 1) as g:
                    for j in range(RING):
                        expert_out(g * RING + j, j)
                for j in range(RING):
                    expert_out(V_SLABS - RING + j, j, final=(j == RING - 1))
                for b in range(TB):
                    for half in range(2):
                        pe.wait_ge((y_ready, y_act_ready)[b], layer * 2 + half + 1)
                        for c in range(4):
                            last = nc.tensor.transpose(pair(4, 8)[:, 4 * half + c, b * P:(b + 1) * P],
                                                       y_nat[:, 2 * b + half, c * P:(c + 1) * P], ident[:])
                last.then_inc(y_mm, 1)
            mean_square(DEPTH * NORMS + 1)



def kernel(x, mem, g_mix, w_in, b_if, conv_w, conv_b, g_head, w_out, g_xattn, g_mem,
           w_xq, w_xk, w_xv, w_xo, g_ffn, w_pq, sub_keys, u_experts, v_experts, g_final):
    import numpy as np
    import concourse.bacc as bacc
    from concourse.bass_utils import run_bass_kernel_spmd

    def col(a):
        return np.asarray(a).reshape(DEPTH, -1, P).transpose(0, 2, 1)

    def slab(w):
        w = np.asarray(w)
        return w.reshape(DEPTH, KB, P, -1, P).transpose(0, 3, 2, 1, 4).reshape(DEPTH, -1, P, D)

    w_in = np.asarray(w_in)
    cols = IN_SLABS * P
    parts = [slab(w_in[:, :, :cols]), slab(w_xk), slab(w_xv), slab(w_out), slab(w_xq), slab(w_xo), slab(w_pq),
             np.asarray(u_experts).reshape(DEPTH, NKEYS, NKEYS, KB, P).transpose(0, 1, 4, 3, 2).reshape(DEPTH, NKEYS, P, D),
             np.asarray(v_experts).reshape(DEPTH, NKEYS, P, D)]
    slabs = np.concatenate(parts, axis=1).reshape(DEPTH * SLABS, P, D)
    w_if = w_in[:, :, cols:].reshape(DEPTH, KB, P, 8).transpose(0, 2, 1, 3).reshape(DEPTH, P, KB * 8)
    cw = np.asarray(conv_w)
    params = np.concatenate([col(g_mix), col(g_mem), col(g_xattn), col(g_ffn), col(g_head),
                             col(cw.reshape(DEPTH, -1)), col(conv_b),
                             np.broadcast_to(np.asarray(b_if)[:, None, :], (DEPTH, P, 8)), w_if], axis=2)
    arrays = {
        "x": np.asarray(x)[0].reshape(T, KB, P).transpose(2, 1, 0),
        "mem": np.asarray(mem)[0].reshape(NMEM, KB, P).transpose(2, 1, 0),
        "slabs": slabs,
        "params": params,
        "g_final": np.asarray(g_final).reshape(KB, P).transpose(1, 0),
        "sub_keys": np.asarray(sub_keys).reshape(DEPTH, SETS, NKEYS, P).transpose(0, 3, 1, 2),
    }
    arrays = {name: np.ascontiguousarray(a) for name, a in arrays.items()}
    nc = bacc.Bacc("TRN2", target_bir_lowering=False, num_devices=1)
    args = [nc.dram_tensor(name, a.shape, FP32, kind="ExternalInput").ap() for name, a in arrays.items()]
    out = nc.dram_tensor("out", (P, KB, T), FP32, kind="ExternalOutput").ap()
    trunk(nc, *args, out)
    got = run_bass_kernel_spmd(nc, [arrays], core_ids=[0]).results[0]["out"]
    return got.transpose(2, 1, 0).reshape(1, T, D)
```

```python
from contextlib import ExitStack

import concourse.bass as bass
from concourse import mybir

FP32 = mybir.dt.float32
F32R = mybir.dt.float32r
U32 = mybir.dt.uint32
ALU = mybir.AluOpType
ACT = mybir.ActivationFunctionType
AX = mybir.AxisListType
ds = bass.ds

P = 128
D = 1024
KB = D // P
T = 256
TB = T // P
NMEM = 256
DEPTH = 2
EPS = 1e-6
LH = 4
LSTM_SCALE = 128 ** -0.5
XH = 4
X_SCALE = 256 ** -0.5
PH = 8
SETS = 2 * PH
TOPK = 16
NKEYS = 128
LOWEST = -3.4028234663852886e38

IN_SLABS, K_SLABS, OUT_SLABS, Q_SLABS, XV_SLABS, XO_SLABS, PQ_SLABS = 28, 8, 8, 8, 8, 8, 16
U_SLABS = V_SLABS = 128
IN_AT = 0
K1_AT = IN_AT + IN_SLABS
OUT_AT = K1_AT + K_SLABS // 2
K2_AT = OUT_AT + OUT_SLABS
Q_AT = K2_AT + K_SLABS // 2
XV_AT = Q_AT + Q_SLABS
XO_AT = XV_AT + XV_SLABS
PQ_AT = XO_AT + XO_SLABS
U_AT = PQ_AT + PQ_SLABS
V_AT = U_AT + U_SLABS
SLABS = V_AT + V_SLABS
Z_Q, Z_K, Z_V, Z_O, Z_B, Z_U, Z_C = range(0, IN_SLABS, 4)
Z_ORDER = (12, 16, 20, 24, 0, 8, 4)
RING = 4
IN_EV, K_EV = 0, IN_SLABS
Q_EV = K_EV + K_SLABS
PQ_EV = Q_EV + Q_SLABS
U_EV = PQ_EV + PQ_SLABS
ACT_EVS = U_EV + U_SLABS
DVE_EVS = OUT_SLABS + XO_SLABS

G_MIX, G_MEM, G_XATTN, G_FFN = 0, 8, 16, 24
G_HEAD, CONV_W, CONV_B, B_IF, W_IF = 32, 36, 48, 52, 60
N_PARAM = W_IF + KB * 8

USE_MIX, USE_MEM, USE_Y, USE_XATTN, USE_AO, USE_FFN, USES = range(7)
XN_INDEX = {USE_MIX: 0, USE_MEM: 1, USE_Y: 2, USE_XATTN: 3, USE_FFN: 4}
XN_USES = len(XN_INDEX)
CHUNKED = 2 * KB
NORM_MIX, NORM_MEM, NORM_XATTN, NORM_FFN, NORMS = range(5)
WHOLE = 2

KEYS_READ = 64
RETRIEVED = 88
POOL_TOKENS = (3, 2, 3, 2)
GROUPS = T // 4


class Steps:

    def __init__(self, eng, sem):
        self.eng, self.sem, self.n = eng, sem, 0

    def mark(self, ins):
        ins.then_inc(self.sem, 1)
        self.n += 1

    def join(self):
        self.eng.wait_ge(self.sem, self.n)

    def link(self, ins):
        self.mark(ins)
        self.join()

    def restart(self):
        self.join()
        self.eng.sem_clear(self.sem)
        self.n = 0


def trunk(nc, x, mem, slabs, params, g_final, sub_keys, out):
    ctx = ExitStack()
    with ctx:
        base = (nc.sbuf_base + 63) // 64 * 64
        limit = nc.sbuf_usable_end
        ctx.enter_context(nc.sbuf_tensor("arena", [P, (limit - base - 64) // 4], FP32))
        top = [base]

        def at(name, offset, shape, dt=FP32):
            return nc.alloc_sbuf_tensor_at(name, shape, dt, offset=offset)

        def sb(name, shape, dt=FP32):
            size = 4
            for n in shape[1:]:
                size *= n
            t = at(name, top[0], shape, dt)
            top[0] += (size + 31) // 32 * 32
            assert top[0] <= limit, name
            return t

        raw = sb("raw", [P, RING, D])
        w_hi = sb("w_hi", [P, RING, KB, P], F32R)
        w_lo = sb("w_lo", [P, RING, KB, P], F32R)
        xT = sb("xT", [P, KB, T])
        act_at = top[0]
        act_hi = sb("act_hi", [P, KB, T], F32R)
        act_lo = sb("act_lo", [P, KB, T], F32R)
        hot_col = at("hot_col", act_at, [P, RING, 4, P])
        y_nat = at("y_nat", act_at, [P, 4, 512])
        hot_row = at("hot_row", act_at + RING * 4 * P * 4, [P, RING, 4, P])
        ident = sb("ident", [P, P])
        eps = sb("eps", [P, 1])
        ones = sb("ones", [P, P])
        tri = sb("tri", [P, P])
        iota = sb("iota", [P, P])
        par = sb("par", [P, N_PARAM])
        gfin = sb("gfin", [P, KB])
        wif_hi = sb("wif_hi", [P, KB, 8], F32R)
        wif_lo = sb("wif_lo", [P, KB, 8], F32R)
        rowT = sb("rowT", [P, T])
        colT = sb("colT", [P, T])
        gateT = sb("gateT", [P, T])
        cols16 = sb("cols16", [P, 4 * RING])
        gated_at = top[0]
        gated = sb("gated", [P, NKEYS, T])

        def tmp(name, kib, shape, dt=FP32):
            size = 4
            for n in shape[1:]:
                size *= n
            assert kib * 1024 + size <= NKEYS * T * 4, name
            return at(name, gated_at + int(kib * 1024), shape, dt)

        memT = tmp("memT", 0, [P, KB, NMEM])
        mem_lo = tmp("mem_lo", 0, [P, KB, NMEM], F32R)
        mem_hi = tmp("mem_hi", 120, [P, KB, NMEM], F32R)
        kT = tmp("kT", 8, [P, K_SLABS, NMEM])
        v_mem = tmp("v_mem", 24, [P, 2, D])
        zT = tmp("zT", 32, [P, IN_SLABS, T])
        u_pad = tmp("u_pad", 60, [P, 4, T + 2])
        conv = tmp("conv", 65, [P, 4, T])
        v_nat = tmp("v_nat", 69, [P, TB, LH, P])
        arg = tmp("arg", 73, [P, LH, 384])
        s_w = tmp("s_w", 79, [P, LH, 384])
        den = tmp("den", 85, [P, LH, T])
        hl = tmp("hl", 89, [P, LH, T])
        o_sig = tmp("o_sig", 93, [P, LH, T])
        gates = tmp("gates", 97, [P, TB, 8])
        nf = tmp("nf", 97.25, [P, TB, 4])
        ef = tmp("ef", 97.5, [P, TB, 4])
        ls = tmp("ls", 97.75, [P, TB, 4])
        b_nat = tmp("b_nat", 98, [P, TB, 4])
        r_nat = tmp("r_nat", 98.25, [P, TB, 4])
        mf = tmp("mf", 98.5, [P, TB, 4])
        r_row = tmp("r_row", 99, [4, T])
        m_row = tmp("m_row", 100, [4, T])
        e_row = tmp("e_row", 101, [4, T])
        rstd = tmp("rstd", 102, [P, T])
        sq = tmp("sq", 104, [P, KB, T])
        e_bc = tmp("e_bc", 104, [P, LH, T])
        xn = tmp("xn", 112, [P, KB, T])
        skT = tmp("skT", 120, [P, SETS, NKEYS])
        qT = tmp("qT", 32, [P, KB, T])
        prob = tmp("prob", 40, [P, 2 * XH, NMEM])
        probT = tmp("probT", 48, [P, 2, XH, T])
        rmax = tmp("rmax", 97, [P, 8])
        nmax = tmp("nmax", 97.25, [P, 8])
        rsum = tmp("rsum", 97.5, [P, 8])
        rinv = tmp("rinv", 97.75, [P, 8])
        qpT = tmp("qpT", 64, [P, SETS, T])
        scores1 = tmp("scores1", 64, [P, SETS, NKEYS])
        scores0 = tmp("scores0", 80, [P, SETS, NKEYS])
        top_v = tmp("top_v", RETRIEVED, [P, TB * SETS, TOPK])
        top_i = tmp("top_i", 90, [P, TB * SETS, TOPK])
        fin_v = tmp("fin_v", 92, [P, TB * PH, TOPK])
        fin_i = tmp("fin_i", 93, [P, TB * PH, TOPK], U32)
        a_u = tmp("a_u", 94, [P, TB * PH * TOPK], U32)
        b_u = tmp("b_u", 95, [P, TB * PH * TOPK], U32)
        a_f = tmp("a_f", 96, [P, TB * PH * TOPK])
        b_f = tmp("b_f", 97, [P, TB * PH * TOPK])
        row_f = tmp("row_f", 98, [P, TB * PH * TOPK])
        col_f = tmp("col_f", 99, [P, TB * PH * TOPK])
        g_exp = tmp("g_exp", 100, [P, TB * PH, TOPK])
        g_sum = tmp("g_sum", 101, [P, TB * PH])
        pick = tmp("pick", 104, [P, TB * PH * TOPK, TOPK])
        top_u = tmp("top_u", 104, [P, TB * SETS, TOPK], U32)
        cand = tmp("cand", 106, [P, 2, TOPK * TOPK])
        struck = tmp("struck", 108, [P, 2, TOPK * TOPK])

        ps = ctx.enter_context(nc.psum_tensor("ps", [P, 8, 512], FP32))

        def pair(b0, n):
            return ps[:, b0:b0 + n // 2, :].rearrange("p b (i t) -> p (b i) t", i=2)

        def sem(name):
            return ctx.enter_context(nc.semaphore(name))

        raw_loaded = [sem(f"raw_loaded{j}") for j in range(RING)]
        hi_ready, lo_ready, slab_done = sem("hi_ready"), sem("lo_ready"), sem("slab_done")
        act_evac, dve_evac = sem("act_evac"), sem("dve_evac")
        x_loaded, x_ffn, par_loaded = sem("x_loaded"), sem("x_ffn"), sem("par_loaded")
        mem_loaded, keys_loaded, out_stored = sem("mem_loaded"), sem("keys_loaded"), sem("out_stored")
        consts, const_step, pool_step = sem("consts"), sem("const_step"), sem("pool_step")
        sq_ready, ms_ready, xn_ready = sem("sq_ready"), sem("ms_ready"), sem("xn_ready")
        root_ready, hroot_ready, abs_ready = sem("root_ready"), sem("hroot_ready"), sem("abs_ready")
        act_hi_ready, act_ready = sem("act_hi_ready"), sem("act_ready")
        wif_hi_ready, wif_ready, gates_mm = sem("wif_hi_ready"), sem("wif_ready"), sem("gates_mm")
        nf_ready, lnf_ready, ls_ready = sem("nf_ready"), sem("lnf_ready"), sem("ls_ready")
        cum_ready, r_ready, rows_mm = sem("cum_ready"), sem("r_ready"), sem("rows_mm")
        eb_ready, e_ready, bc_mm, e_bc_ready = sem("eb_ready"), sem("e_ready"), sem("bc_mm"), sem("e_bc_ready")
        v_tr, v_nat_ready = sem("v_tr"), sem("v_nat_ready")
        vmem_act, vmem_dve, sq_chunk = sem("vmem_act"), sem("vmem_dve"), sem("sq_chunk")
        o_ready, qk_mm, arg_ready, dw_ready = sem("o_ready"), sem("qk_mm"), sem("arg_ready"), sem("dw_ready")
        s_ready, nd_mm, hl_ready, hsq_ready, hms_mm = (sem("s_ready"), sem("nd_mm"), sem("hl_ready"),
                                                      sem("hsq_ready"), sem("hms_mm"))
        xs_mm, nmax_ready, exp_ready, prob_ready = sem("xs_mm"), sem("nmax_ready"), sem("exp_ready"), sem("prob_ready")
        pt_mm, pt_dve, pt_act, xo_mm = sem("pt_mm"), sem("pt_dve"), sem("pt_act"), sem("xo_mm")
        sc_mm, sc_evac, fin_ready, gexp_ready = sem("sc_mm"), sem("sc_evac"), sem("fin_ready"), sem("gexp_ready")
        keys_read, decoded, ret_mm, cols_ready = sem("keys_read"), sem("decoded"), sem("ret_mm"), sem("cols_ready")
        hot_act_ready, y_ready, y_act_ready, y_mm = sem("hot_act_ready"), sem("y_ready"), sem("y_act_ready"), sem("y_mm")
        hot_col_ready, hot_row_ready, gate_mm = sem("hot_col_ready"), sem("hot_row_ready"), sem("gate_mm")
        gated_ready, ga_hi_ready, ga_ready = sem("gated_ready"), sem("ga_hi_ready"), sem("ga_ready")
        settled = sem("settled")
        act_step, dve_step, out_ready = sem("act_step"), sem("dve_step"), sem("out_ready")

        def settle(eng):
            eng.sem_inc(settled, 1)

        block = ctx.enter_context(nc.Block())

        @block.sync
        def _(sp):
            def load(j, slab):
                sp.dma_start(raw[:, j, :], slab).then_inc(raw_loaded[j], 16)

            sp.dma_start(xT[:], x).then_inc(x_loaded, 16)
            sp.dma_start(gfin[:], g_final).then_inc(x_loaded, 16)
            for j in range(RING):
                load(j, slabs[j])
            with sp.Fori(1, DEPTH * SLABS // RING) as g:
                for j in range(RING):
                    sp.wait_ge(lo_ready, g * RING + (j - RING + 1))
                    load(j, slabs[ds(g * RING + j, 1)].rearrange("o p f -> (o p) f"))
            for j in range(RING):
                sp.wait_ge(lo_ready, DEPTH * SLABS - RING + j + 1)
                load(j, slabs[j])
            sp.wait_ge(out_ready, 1)
            sp.dma_start(out, xn[:]).then_inc(out_stored, 16)
            sp.wait_ge(out_stored, 16)

        @block.gpsimd
        def _(pool):
            nc.gpsimd.memset(ident[:], 0.0).then_inc(const_step, 1)
            nc.gpsimd.memset(ones[:], 1.0).then_inc(const_step, 1)
            nc.gpsimd.memset(eps[:], EPS).then_inc(consts, 1)
            pool.wait_ge(const_step, 2)
            nc.gpsimd.affine_select(out=ident[:], in_=ident[:], compare_op=ALU.not_equal, fill=1.0,
                                    base=0, pattern=[[-1, P]], channel_multiplier=1).then_inc(consts, 1)
            nc.gpsimd.affine_select(out=tri[:], in_=ones[:], compare_op=ALU.is_ge, fill=0.0,
                                    base=0, pattern=[[1, P]], channel_multiplier=-1).then_inc(consts, 1)
            nc.gpsimd.iota(iota[:], [[1, P]], base=0, channel_multiplier=0,
                           allow_small_or_imprecise_dtypes=True).then_inc(consts, 1)
            with pool.Fori(0, DEPTH) as layer:
                pool.wait_ge(x_ffn, layer + 1)
                pool.dma_start(par[:], params[ds(layer, 1)].rearrange("o p f -> (o p) f")).then_inc(par_loaded, 16)
                pool.dma_start(memT[:], mem).then_inc(mem_loaded, 16)
                pool.wait_ge(slab_done, layer * SLABS + XO_AT)
                pool.dma_start(skT[:], sub_keys[ds(layer, 1)].rearrange("o p s k -> (o p) s k")).then_inc(keys_loaded, 16)
                pool.wait_ge(cols_ready, layer + 1)
                pool.wait_ge(slab_done, layer * SLABS + V_AT)
                settle(pool)
                with pool.Fori(0, GROUPS // RING) as g:
                    nc.gpsimd.tensor_copy(cols16[:], colT[:, ds(g * (4 * RING), 4 * RING)]).then_inc(pool_step, 1)
                    pool.wait_ge(pool_step, layer * (GROUPS // RING) + g + 1)
                    for s in range(RING):
                        pool.wait_ge(gate_mm, layer * GROUPS + g * RING + s + 1)
                        settle(pool)
                        for i in range(POOL_TOKENS[s]):
                            last = nc.gpsimd.tensor_scalar(hot_col[:, s, i, :], iota[:],
                                                           cols16[:, 4 * s + i:4 * s + i + 1], None, ALU.is_equal)
                        last.then_inc(hot_col_ready, 1)
                    pool.wait_ge(hot_col_ready, layer * GROUPS + g * RING + RING)

        @block.scalar
        def _(act):
            step = Steps(act, act_step)

            def turn(layer, at0, g, j, evac):
                act.wait_ge(slab_done, layer * SLABS + at0 + g * RING + j + 1)
                if evac is not None:
                    evac(j, g * RING + j).then_inc(act_evac, 1)
                act.wait_ge(raw_loaded[j], (layer * (SLABS // RING) + (at0 // RING + 2) + g) * 16)
                nc.scalar.activation(w_hi[:, j].rearrange("p k c -> p (k c)"), raw[:, j, :],
                                     ACT.Copy).then_inc(hi_ready, 1)

            def group(layer, at0, evac=None, slots=range(RING)):
                for j in slots:
                    turn(layer, at0, 0, j, evac)

            def section(layer, at0, slabs_n, evac=None):
                with act.Fori(0, slabs_n // RING) as g:
                    for j in range(RING):
                        turn(layer, at0, g, j, evac)

            def copy_to(dst, first=0):
                return lambda j, n: nc.scalar.activation(dst[:, ds(n + first, 1), :], ps[:, j:j + 1, 0:T], ACT.Copy)

            def squares(src):
                nc.scalar.activation(sq[:], src[:], ACT.Square, scale=D ** -0.5).then_inc(sq_ready, 1)

            def roots(count):
                act.wait_ge(ms_ready, count)
                nc.scalar.activation(rstd[:], ps[:, 7, 0:T], ACT.Sqrt, bias=eps[:]).then_inc(root_ready, 1)

            def x_group(layer, at0, ev):
                for n in range(KB):
                    turn(layer, at0 + n // RING * RING, 0, n % RING, None)
                    act.wait_ge(dve_evac, layer * DVE_EVS + ev + RING + n + 1)
                    nc.scalar.activation(sq[:, n, :], xT[:, n, :], ACT.Square, scale=D ** -0.5).then_inc(sq_chunk, 1)

            def operand_hi(layer, use, free_at=None, dst=act_hi, order=(0, 1)):
                if free_at is not None:
                    act.wait_ge(slab_done, layer * SLABS + free_at)
                for i, half in enumerate(order):
                    act.wait_ge(xn_ready, layer * (2 * XN_USES) + 2 * XN_INDEX[use] + i + 1)
                    nc.scalar.activation(dst[:, 4 * half:4 * half + 4], xn[:, 4 * half:4 * half + 4],
                                         ACT.Copy).then_inc(act_hi_ready, 1)

            act.wait_ge(consts, 4)
            nc.scalar.sem_inc(act_evac, RING)
            for j in range(RING):
                act.wait_ge(raw_loaded[j], 16)
                nc.scalar.activation(w_hi[:, j].rearrange("p k c -> p (k c)"), raw[:, j, :],
                                     ACT.Copy).then_inc(hi_ready, 1)
            with act.Fori(0, DEPTH) as layer:
                act.wait_ge(x_ffn, layer + 1)
                squares(xT)
                roots(layer * NORMS + NORM_MIX + 1)
                act.wait_ge(par_loaded, layer * 16 + 16)
                nc.scalar.activation(wif_hi[:].rearrange("p k c -> p (k c)"), par[:, W_IF:W_IF + KB * 8],
                                     ACT.Copy).then_inc(wif_hi_ready, 1)
                operand_hi(layer, USE_MIX)
                act.wait_ge(mem_loaded, layer * 16 + 16)
                squares(memT)
                act.wait_ge(nf_ready, layer + 1)
                step.link(nc.scalar.activation(ef[:], nf[:], ACT.Exp))
                nc.scalar.activation(ef[:], ef[:], ACT.Ln, bias=1.0).then_inc(lnf_ready, 1)
                step.restart()
                group(layer, Z_Q, copy_to(zT, Z_Q))
                roots(layer * NORMS + NORM_MEM + 1)
                group(layer, Z_K, copy_to(zT, Z_K))
                operand_hi(layer, USE_MEM, dst=mem_hi)
                act.wait_ge(eb_ready, layer + 1)
                nc.scalar.activation(e_row[:], e_row[:], ACT.Exp, scale=-1.0).then_inc(e_ready, 1)
                group(layer, Z_V, copy_to(zT, Z_V))
                act.wait_ge(bc_mm, layer + 1)
                nc.scalar.activation(e_bc[:], pair(4, 4), ACT.Copy).then_inc(e_bc_ready, 1)
                act.wait_ge(arg_ready, layer + 1)
                nc.scalar.activation(arg[:], arg[:], ACT.Exp, scale=-1.0).then_inc(dw_ready, 1)
                group(layer, Z_O, copy_to(zT, Z_O))
                act.wait_ge(v_tr, layer + 1)
                nc.scalar.activation(v_nat[:].rearrange("p b h c -> p (b h c)"),
                                     ps[:, 4:6, :].rearrange("p b c -> p (b c)"), ACT.Copy).then_inc(v_nat_ready, 1)
                act.wait_ge(act_evac, layer * ACT_EVS + Z_O + 4 + RING)
                nc.scalar.activation(o_sig[:], zT[:, Z_O:Z_O + 4, :], ACT.Sigmoid).then_inc(o_ready, 1)
                group(layer, Z_B, copy_to(zT, Z_B))
                group(layer, Z_U, copy_to(zT, Z_U))
                act.wait_ge(nd_mm, layer + 1)
                nc.scalar.activation(den[:], pair(6, 4), ACT.Abs).then_inc(abs_ready, 1)
                group(layer, Z_C, copy_to(zT, Z_C), (0, 1))
                act.wait_ge(hl_ready, layer + 1)
                nc.scalar.activation(den[:], hl[:], ACT.Square).then_inc(hsq_ready, 1)
                group(layer, Z_C, copy_to(zT, Z_C), (2, 3))
                act.wait_ge(hms_mm, layer + 1)
                nc.scalar.activation(o_sig[:], pair(6, 4), ACT.Sqrt, bias=eps[:], scale=1.0 / P).then_inc(hroot_ready, 1)
                group(layer, K1_AT, copy_to(kT), (0, 1))
                operand_hi(layer, USE_Y, K1_AT, order=(1, 0))
                group(layer, K1_AT, copy_to(kT), (2, 3))
                x_group(layer, OUT_AT, 0)
                roots(layer * NORMS + NORM_XATTN + 1)
                operand_hi(layer, USE_XATTN, K2_AT)
                group(layer, K2_AT, copy_to(kT, 4))
                section(layer, Q_AT, Q_SLABS, copy_to(qT))
                act.wait_ge(nmax_ready, layer + 1)
                for i in range(2 * XH):
                    last = nc.scalar.activation(prob[:, i, :], pair(4, 8)[:, i, :], ACT.Exp, bias=nmax[:, i:i + 1],
                                                scale=X_SCALE, accum_out=rsum[:, i:i + 1])
                last.then_inc(exp_ready, 1)
                group(layer, XV_AT)
                act.wait_ge(pt_mm, layer + 1)
                nc.scalar.activation(probT[:, 1], pair(6, 4), ACT.Copy).then_inc(pt_act, 1)
                group(layer, XV_AT + RING)
                act.wait_ge(slab_done, layer * SLABS + XO_AT)
                nc.scalar.activation(v_mem[:, 1, :], ps[:, 2:4, :].rearrange("p b c -> p (b c)"),
                                     ACT.Copy).then_inc(vmem_act, 1)
                for half in range(2):
                    act.wait_ge(xo_mm, layer * 2 + half + 1)
                    nc.scalar.activation(act_hi[:, 4 * half:4 * half + 4], pair(4 + 2 * half, 4),
                                         ACT.Copy).then_inc(act_hi_ready, 1)
                x_group(layer, XO_AT, OUT_SLABS)
                roots(layer * NORMS + NORM_FFN + 1)
                operand_hi(layer, USE_FFN, PQ_AT)
                section(layer, PQ_AT, PQ_SLABS, copy_to(qpT))

                def gelu_to(first):
                    return lambda j, n: nc.scalar.activation(gated[:, ds(n + first, 1), :], ps[:, j:j + 1, 0:T], ACT.Gelu)

                def scores_out(b, dst):
                    act.wait_ge(sc_mm, layer * TB + b + 1)
                    nc.scalar.activation(dst[:].rearrange("p n k -> p (n k)"),
                                         ps[:, 4:8, :].rearrange("p b c -> p (b c)"), ACT.Copy).then_inc(sc_evac, 1)

                scores_out(0, scores0)
                section(layer, U_AT, RING, gelu_to(0))
                scores_out(1, scores1)
                section(layer, U_AT + RING, KEYS_READ - RING, gelu_to(RING))
                act.wait_ge(keys_read, layer + 1)
                section(layer, U_AT + KEYS_READ, RING, gelu_to(KEYS_READ))
                act.wait_ge(fin_ready, layer + 1)
                nc.scalar.activation(g_exp[:], g_exp[:], ACT.Exp).then_inc(gexp_ready, 1)
                section(layer, U_AT + KEYS_READ + RING, RETRIEVED - KEYS_READ - RING, gelu_to(KEYS_READ + RING))
                act.wait_ge(ret_mm, layer + 1)
                section(layer, U_AT + RETRIEVED, U_SLABS - RETRIEVED, gelu_to(RETRIEVED))

                def gated_hi(j, n):
                    nc.scalar.activation(act_hi[:, j:j + 1, :], gated[:, n, :], ACT.Copy).then_inc(ga_hi_ready, 1)

                act.wait_ge(cols_ready, layer + 1)
                settle(act)
                with act.Fori(0, GROUPS // RING) as g:
                    for s in range(RING):
                        first = POOL_TOKENS[s]
                        act.wait_ge(gate_mm, layer * GROUPS + g * RING + s + 1)
                        settle(act)
                        for i in range(first, 4):
                            last = nc.scalar.activation(hot_col[:, s, i, :], iota[:], ACT.Abs, scale=-1.0,
                                                        bias=colT[:, ds(g * (4 * RING) + 4 * s + i, 1)])
                        step.mark(last)
                        if s % 2 == 1:
                            step.join()
                            for q in (s - 1, s):
                                first = POOL_TOKENS[q]
                                nc.scalar.activation(hot_col[:, q, first:4, :], hot_col[:, q, first:4, :], ACT.Relu,
                                                     scale=-1.0, bias=ones[:, 0:1]).then_inc(hot_act_ready, 1)
                    step.restart()
                act.wait_ge(gated_ready, layer + 1)
                for j in range(RING):
                    gated_hi(j, slice(j, j + 1))
                with act.Fori(0, V_SLABS // RING - 1) as g:
                    for j in range(RING):
                        act.wait_ge(slab_done, layer * SLABS + V_AT + g * RING + j + 1)
                        act.wait_ge(raw_loaded[j], (layer * (SLABS // RING) + (V_AT // RING + 2) + g) * 16)
                        nc.scalar.activation(w_hi[:, j].rearrange("p k c -> p (k c)"), raw[:, j, :],
                                             ACT.Copy).then_inc(hi_ready, 1)
                        gated_hi(j, ds(g * RING + RING + j, 1))
                for j in range(RING):
                    act.wait_ge(slab_done, layer * SLABS + SLABS - RING + j + 1)
                    act.wait_ge(raw_loaded[j], (layer + 1) * (SLABS // RING * 16) + 16)
                    nc.scalar.activation(w_hi[:, j].rearrange("p k c -> p (k c)"), raw[:, j, :],
                                         ACT.Copy).then_inc(hi_ready, 1)
                act.wait_ge(slab_done, layer * SLABS + SLABS)
                for i in range(2, 4):
                    nc.scalar.activation(y_nat[:, i, :], ps[:, i, :], ACT.Copy).then_inc(y_act_ready, 1)
            act.wait_ge(x_ffn, DEPTH + 1)
            squares(xT)
            roots(DEPTH * NORMS + 1)

        @block.vector
        def _(dve):
            step = Steps(dve, dve_step)

            def lo_part(layer, at0, g, j):
                dve.wait_ge(hi_ready, layer * SLABS + at0 + g * RING + j + 1)
                nc.vector.tensor_tensor(w_lo[:, j].rearrange("p k c -> p (k c)"), raw[:, j, :],
                                        w_hi[:, j].rearrange("p k c -> p (k c)").bitcast(FP32),
                                        ALU.subtract).then_inc(lo_ready, 1)

            def group(layer, at0, slots=range(RING)):
                for j in slots:
                    lo_part(layer, at0 + RING, 0, j)

            def x_group(layer, at0):
                for n in range(KB):
                    dve.wait_ge(slab_done, layer * SLABS + at0 + n + 1)
                    add_to_x(n % RING, n).then_inc(dve_evac, 1)
                    lo_part(layer, at0 + RING + n // RING * RING, 0, n % RING)

            def section(layer, at0, slabs_n, evac=None):
                with dve.Fori(0, slabs_n // RING) as g:
                    for j in range(RING):
                        if evac is not None:
                            dve.wait_ge(slab_done, layer * SLABS + at0 + g * RING + j + 1)
                            evac(j, g * RING + j).then_inc(dve_evac, 1)
                        lo_part(layer, at0 + RING, g, j)

            def add_to_x(j, n):
                return nc.vector.tensor_tensor(xT[:, ds(n, 1), :], xT[:, ds(n, 1), :], ps[:, j:j + 1, 0:T], ALU.add)

            def norm(src, g_col, norm_count, half_done):
                dve.wait_ge(root_ready, norm_count)
                step.link(nc.vector.reciprocal(rstd[:], rstd[:]))
                for half in range(2):
                    for k in range(4 * half, 4 * half + 4):
                        last = nc.vector.scalar_tensor_tensor(xn[:, k, :], src[:, k, :], g_col[:, k:k + 1], rstd[:],
                                                              ALU.mult, ALU.mult)
                    half_done(last)

            def operand_lo(layer, use, hi=act_hi, lo=act_lo, order=(0, 1)):
                for i, half in enumerate(order):
                    h = slice(4 * half, 4 * half + 4)
                    dve.wait_ge(act_hi_ready, layer * (2 * USES) + 2 * use + i + 1)
                    nc.vector.tensor_tensor(lo[:, h], pair(4 + 2 * half, 4) if use == USE_AO else xn[:, h],
                                            hi[:, h].bitcast(FP32), ALU.subtract).then_inc(act_ready, 1)

            def to_xn(ins):
                ins.then_inc(xn_ready, 1)

            nc.vector.sem_inc(dve_evac, RING)
            dve.wait_ge(x_loaded, 32)
            nc.vector.sem_inc(x_ffn, 1)
            for j in range(RING):
                dve.wait_ge(hi_ready, j + 1)
                nc.vector.tensor_tensor(w_lo[:, j].rearrange("p k c -> p (k c)"), raw[:, j, :],
                                        w_hi[:, j].rearrange("p k c -> p (k c)").bitcast(FP32),
                                        ALU.subtract).then_inc(lo_ready, 1)
            dve.wait_ge(consts, 4)
            with dve.Fori(0, DEPTH) as layer:
                dve.wait_ge(wif_hi_ready, layer + 1)
                nc.vector.tensor_tensor(wif_lo[:].rearrange("p k c -> p (k c)"), par[:, W_IF:W_IF + KB * 8],
                                        wif_hi[:].rearrange("p k c -> p (k c)").bitcast(FP32),
                                        ALU.subtract).then_inc(wif_ready, 1)
                norm(xT, par[:, G_MIX:G_MIX + 8], layer * NORMS + NORM_MIX + 1, to_xn)
                operand_lo(layer, USE_MIX)
                dve.wait_ge(gates_mm, layer + 1)
                step.link(nc.vector.tensor_tensor(
                    gates[:], ps[:, 4, 0:16].rearrange("p (b c) -> p b c", b=TB),
                    par[:, B_IF:B_IF + 8].unsqueeze(1).to_broadcast([P, TB, 8]), ALU.add))
                nc.vector.scalar_tensor_tensor(nf[:], gates[:, :, 4:8], -1.0, gates[:, :, 4:8], ALU.mult, ALU.min).then_inc(nf_ready, 1)
                step.mark(nc.vector.tensor_scalar(mf[:], gates[:, :, 4:8], 0.0, None, ALU.min))
                dve.wait_ge(lnf_ready, layer + 1)
                step.join()
                nc.vector.tensor_tensor(ls[:], mf[:], ef[:], ALU.subtract).then_inc(ls_ready, 1)
                group(layer, Z_Q)
                dve.wait_ge(cum_ready, layer + 1)
                step.link(nc.vector.tensor_copy(b_nat[:], ps[:, 6, 0:8].rearrange("p (b h) -> p b h", b=TB)))
                nc.vector.tensor_tensor(r_nat[:], gates[:, :, 0:4], b_nat[:], ALU.subtract).then_inc(r_ready, 1)
                norm(memT, par[:, G_MEM:G_MEM + 8], layer * NORMS + NORM_MEM + 1, to_xn)
                group(layer, Z_K)
                dve.wait_ge(rows_mm, layer + 1)
                step.link(nc.vector.tensor_copy(r_row[:], ps[0:4, 5, 0:T]))
                step.link(nc.vector.tensor_tensor_scan(m_row[:], r_row[:], r_row[:], 0.0, ALU.max, ALU.max))
                nc.vector.tensor_tensor(e_row[:], m_row[:], ps[0:4, 5, T:2 * T], ALU.add).then_inc(eb_ready, 1)
                operand_lo(layer, USE_MEM, mem_hi, mem_lo)
                group(layer, Z_V)
                dve.wait_ge(bc_mm, layer + 1)
                for h in range(LH):
                    m_bc = pair(6, 4)[:, h, :]
                    nc.vector.tensor_scalar(arg[:, h, 0:T], m_bc, r_nat[:, 0, h:h + 1], 0.0, ALU.subtract, ALU.max)
                    last = nc.vector.tensor_scalar(arg[:, h, T:384], m_bc[:, P:T], r_nat[:, 1, h:h + 1], 0.0,
                                                   ALU.subtract, ALU.max)
                last.then_inc(arg_ready, 1)
                group(layer, Z_O)
                dve.wait_ge(dw_ready, layer + 1)
                diag = arg[:].rearrange("p h (i t) -> p h i t", i=3)[:, :, 0:3:2, :]
                step.link(nc.vector.tensor_tensor(diag, diag, tri[:].unsqueeze(1).unsqueeze(1).to_broadcast([P, LH, 2, P]),
                                                  ALU.mult))
                nc.vector.memset(u_pad[:, :, 0:2], 0.0)
                group(layer, Z_B)
                dve.wait_ge(qk_mm, layer + 1)
                for h in range(LH):
                    last = nc.vector.scalar_tensor_tensor(s_w[:, h, :], ps[:, 4 + h, 0:384], LSTM_SCALE, arg[:, h, :],
                                                          ALU.mult, ALU.mult)
                last.then_inc(s_ready, 1)
                group(layer, Z_U)
                dve.wait_ge(abs_ready, layer + 1)
                step.link(nc.vector.tensor_tensor(den[:], den[:], e_bc[:], ALU.max))
                step.link(nc.vector.reciprocal(den[:], den[:]))
                step.link(nc.vector.tensor_tensor(hl[:], pair(4, 4), den[:], ALU.mult))
                dve.wait_ge(o_ready, layer + 1)
                nc.vector.tensor_tensor(hl[:], hl[:], o_sig[:], ALU.mult).then_inc(hl_ready, 1)
                dve.wait_ge(act_evac, layer * ACT_EVS + Z_U + 4 + RING)
                step.link(nc.vector.tensor_tensor(u_pad[:, :, 2:T + 2], zT[:, Z_U:Z_U + 4, :], zT[:, Z_B:Z_B + 4, :], ALU.mult))
                for m in range(4):
                    last = nc.vector.tensor_scalar(conv[:, m, :], u_pad[:, m, 2:T + 2],
                                                   par[:, CONV_W + 8 + m:CONV_W + 9 + m], par[:, CONV_B + m:CONV_B + m + 1],
                                                   ALU.mult, ALU.add)
                step.mark(last)
                group(layer, Z_C, (0, 1))
                step.join()
                for tap in (1, 0):
                    for m in range(4):
                        last = nc.vector.scalar_tensor_tensor(conv[:, m, :], u_pad[:, m, tap:tap + T],
                                                              par[:, CONV_W + 4 * tap + m:CONV_W + 4 * tap + m + 1],
                                                              conv[:, m, :], ALU.mult, ALU.add)
                    step.link(last)
                group(layer, Z_C, (2, 3))
                dve.wait_ge(hroot_ready, layer + 1)
                step.link(nc.vector.reciprocal(o_sig[:], o_sig[:]))
                for h in range(LH):
                    last = nc.vector.scalar_tensor_tensor(xn[:, 4 + h, :], hl[:, h, :], par[:, G_HEAD + h:G_HEAD + h + 1],
                                                          o_sig[:, h, :], ALU.mult, ALU.mult)
                last.then_inc(xn_ready, 1)
                dve.wait_ge(act_evac, layer * ACT_EVS + K_EV + RING)
                nc.vector.tensor_tensor(xn[:, 0:4, :], conv[:], zT[:, Z_C:Z_C + 4, :], ALU.mult).then_inc(xn_ready, 1)
                group(layer, K1_AT, (0, 1))
                operand_lo(layer, USE_Y, order=(1, 0))
                group(layer, K1_AT, (2, 3))
                x_group(layer, OUT_AT)
                norm(xT, par[:, G_XATTN:G_XATTN + 8], layer * NORMS + NORM_XATTN + 1, to_xn)
                operand_lo(layer, USE_XATTN)
                group(layer, K2_AT)
                section(layer, Q_AT, Q_SLABS)
                dve.wait_ge(xs_mm, layer + 1)
                step.link(nc.vector.tensor_reduce(rmax[:], pair(4, 8), AX.X, ALU.max))
                nc.vector.tensor_scalar(nmax[:], rmax[:], -X_SCALE, None, ALU.mult).then_inc(nmax_ready, 1)
                dve.wait_ge(exp_ready, layer + 1)
                step.link(nc.vector.reciprocal(rinv[:], rsum[:]))
                nc.vector.tensor_tensor(prob[:], prob[:], rinv[:].unsqueeze(2).to_broadcast([P, 2 * XH, NMEM]),
                                        ALU.mult).then_inc(prob_ready, 1)
                group(layer, XV_AT)
                dve.wait_ge(pt_mm, layer + 1)
                nc.vector.tensor_copy(probT[:, 0], pair(4, 4)).then_inc(pt_dve, 1)
                group(layer, XV_AT + RING)
                dve.wait_ge(slab_done, layer * SLABS + XO_AT)
                nc.vector.tensor_copy(v_mem[:, 0, :], ps[:, 0:2, :].rearrange("p b c -> p (b c)")).then_inc(vmem_dve, 1)
                operand_lo(layer, USE_AO)
                x_group(layer, XO_AT)
                norm(xT, par[:, G_FFN:G_FFN + 8], layer * NORMS + NORM_FFN + 1, to_xn)
                operand_lo(layer, USE_FFN)
                section(layer, PQ_AT, PQ_SLABS)

                def slab(i):
                    lo_part(layer, U_AT + i - i % RING, 0, i % RING)

                def top16(first, second, beside):
                    rows = (first, second)
                    for src, _, v, _ in rows:
                        step.mark(nc.vector.max(v[:, 0:8], src))
                    slab(beside)
                    step.join()
                    for src, struck, v, i in rows:
                        nc.vector.max_index(i[:, 0:8], v[:, 0:8], src)
                        step.mark(nc.vector.match_replace(struck, v[:, 0:8], src, LOWEST))
                    slab(beside + 1)
                    step.join()
                    for _, struck, v, _ in rows:
                        step.mark(nc.vector.max(v[:, 8:16], struck))
                    step.join()
                    for _, struck, v, i in rows:
                        step.mark(nc.vector.max_index(i[:, 8:16], v[:, 8:16], struck))

                for n in range(0, TB * SETS, 2):
                    if n % SETS == 0:
                        dve.wait_ge(sc_evac, layer * TB + n // SETS + 1)
                        settle(dve)
                    src = (scores0, scores1)[n // SETS]
                    step.join()
                    top16(*[(src[:, m % SETS, :], struck[:, m - n, 0:NKEYS], top_v[:, m, :], top_u[:, m, :])
                            for m in (n, n + 1)], beside=n + RING)
                step.join()
                nc.vector.tensor_copy(top_i[:], top_u[:]).then_inc(keys_read, 1)
                for n in range(0, TB * PH, 2):
                    step.join()
                    for m in (n, n + 1):
                        step.mark(nc.vector.tensor_tensor(
                            cand[:, m - n, :].rearrange("p (a b) -> p a b", a=TOPK),
                            top_v[:, 2 * m, :].unsqueeze(2).to_broadcast([P, TOPK, TOPK]),
                            top_v[:, 2 * m + 1, :].unsqueeze(1).to_broadcast([P, TOPK, TOPK]), ALU.add))
                    slab(RING + TB * SETS + 2 * n)
                    step.join()
                    top16(*[(cand[:, m - n, :], struck[:, m - n, :], fin_v[:, m, :], fin_i[:, m, :])
                            for m in (n, n + 1)], beside=RING + TB * SETS + 2 * n + 1)
                    slab(RING + TB * SETS + 2 * n + 3)
                step.join()
                at_slab = RING + TB * SETS + 2 * TB * PH
                nc.vector.tensor_tensor(g_exp[:], fin_v[:], fin_v[:, :, 0:1].to_broadcast([P, TB * PH, TOPK]),
                                        ALU.subtract).then_inc(fin_ready, 1)
                flat_i = fin_i[:].rearrange("p c k -> p (c k)")
                step.mark(nc.vector.tensor_scalar(a_u[:], flat_i, 4, None, ALU.logical_shift_right))
                step.mark(nc.vector.tensor_scalar(b_u[:], flat_i, 15, None, ALU.bitwise_and))
                slab(at_slab)
                step.join()
                step.mark(nc.vector.tensor_copy(a_f[:], a_u[:]))
                step.mark(nc.vector.tensor_copy(b_f[:], b_u[:]))
                slab(at_slab + 1)
                keys = top_i[:].rearrange("p (c s) a -> p c s a", s=2)
                pick4 = pick[:].rearrange("p (c k) a -> p c k a", k=TOPK)
                n = at_slab + 2
                for side, (place, found) in enumerate(((a_f, row_f), (b_f, col_f))):
                    step.join()
                    step.mark(nc.vector.tensor_tensor(
                        pick[:], place[:].unsqueeze(2).to_broadcast([P, TB * PH * TOPK, TOPK]),
                        iota[:, 0:TOPK].unsqueeze(1).to_broadcast([P, TB * PH * TOPK, TOPK]), ALU.is_equal))
                    for i in range(3):
                        slab(n + i)
                    step.join()
                    step.mark(nc.vector.tensor_tensor(
                        pick4, pick4, keys[:, :, side, :].unsqueeze(2).to_broadcast([P, TB * PH, TOPK, TOPK]), ALU.mult))
                    for i in range(3, 6):
                        slab(n + i)
                    step.join()
                    step.mark(nc.vector.tensor_reduce(found[:], pick[:], AX.X, ALU.add))
                    for i in range(6, 8):
                        slab(n + i)
                    n += 8
                step.join()
                dve.wait_ge(gexp_ready, layer + 1)
                step.mark(nc.vector.tensor_reduce(g_sum[:], g_exp[:], AX.X, ALU.add))
                slab(n)
                step.join()
                step.mark(nc.vector.reciprocal(g_sum[:], g_sum[:]))
                slab(n + 1)
                step.join()
                nc.vector.tensor_tensor(g_exp[:], g_exp[:], g_sum[:].unsqueeze(2).to_broadcast([P, TB * PH, TOPK]),
                                        ALU.mult).then_inc(decoded, 1)
                assert n + 2 == RETRIEVED, n
                section(layer, U_AT + RETRIEVED - RING, RING)
                dve.wait_ge(ret_mm, layer + 1)
                step.mark(nc.vector.tensor_copy(rowT[:], ps[:, 4, 0:T]))
                step.mark(nc.vector.tensor_copy(gateT[:], ps[:, 5, 0:T]))
                nc.vector.tensor_copy(colT[:], ps[:, 4, T:2 * T]).then_inc(cols_ready, 1)
                section(layer, U_AT + RETRIEVED, U_SLABS - RETRIEVED)
                step.join()

                def hot(n, s):
                    dve.wait_ge(gate_mm, layer * GROUPS + n + 1)
                    for i in range(4):
                        t = n * 4 + i
                        last = nc.vector.tensor_scalar(hot_row[:, s, i, :], iota[:], rowT[:, ds(t, 1)],
                                                       gateT[:, ds(t, 1)], ALU.is_equal, ALU.mult)
                    last.then_inc(hot_row_ready, 1)

                def gate(n, s, final=False):
                    dve.wait_ge(gate_mm, layer * GROUPS + n + 1 + RING)
                    g4 = gated[:, :, ds(n * 4, 4)].rearrange("p i t -> p t i")
                    return nc.vector.tensor_tensor(g4, g4, ps[:, 4 + s, :].rearrange("p (t i) -> p t i", t=4), ALU.mult)

                dve.wait_ge(slab_done, layer * SLABS + V_AT)
                hot(0, 0)
                hot(1, 1)
                dve.wait_ge(act_evac, (layer + 1) * ACT_EVS + RING)
                settle(dve)
                with dve.Fori(0, GROUPS // RING - 1) as g:
                    for s in range(RING):
                        hot(g * RING + s + 2, (s + 2) % RING)
                        gate(g * RING + s, s)
                hot(GROUPS - 2, 2)
                gate(GROUPS - 4, 0)
                hot(GROUPS - 1, 3)
                for s in (1, 2, 3):
                    last = gate(GROUPS - 4 + s, s)
                last.then_inc(gated_ready, 1)

                def gated_lo(j, n, ready):
                    dve.wait_ge(ga_hi_ready, ready)
                    nc.vector.tensor_tensor(act_lo[:, j:j + 1, :], gated[:, n, :], act_hi[:, j:j + 1, :].bitcast(FP32),
                                            ALU.subtract).then_inc(ga_ready, 1)

                for j in range(RING):
                    gated_lo(j, slice(j, j + 1), layer * V_SLABS + j + 1)
                with dve.Fori(0, V_SLABS // RING - 1) as g:
                    for j in range(RING):
                        lo_part(layer, V_AT + RING, g, j)
                        gated_lo(j, ds(g * RING + RING + j, 1), layer * V_SLABS + g * RING + RING + j + 1)
                for j in range(RING):
                    lo_part(layer, SLABS, 0, j)
                dve.wait_ge(slab_done, layer * SLABS + SLABS)
                for i in range(2):
                    nc.vector.tensor_copy(y_nat[:, i, :], ps[:, i, :]).then_inc(y_ready, 1)
                dve.wait_ge(y_mm, layer + 1)
                for m in range(4):
                    last = nc.vector.tensor_tensor(xT[:, 2 * m:2 * m + 2, :], xT[:, 2 * m:2 * m + 2, :],
                                                   pair(4, 8)[:, 2 * m:2 * m + 2, :], ALU.add)
                last.then_inc(x_ffn, 1)
                step.restart()
            dve.wait_ge(x_ffn, DEPTH + 1)
            norm(xT, gfin[:], DEPTH * NORMS + 1, step.mark)
            step.join()
            nc.vector.sem_inc(out_ready, 1)

        @block.tensor
        def _(pe):
            PARTS = ((w_hi, act_hi), (w_lo, act_hi), (w_hi, act_lo))

            def slab_product(j, hi, lo):
                for k in range(KB):
                    for i, (w, a) in enumerate(((w_hi, hi), (w_lo, hi), (w_hi, lo))):
                        last = nc.tensor.matmul(ps[:, j, 0:T], w[:, j, k, :], a[:, k, :],
                                                start=(k == 0 and i == 0), stop=(k == KB - 1 and i == 2))
                last.then_inc(slab_done, 1)

            def project(layer, at0, slabs_n, evac, ev_at, ev_per_layer):
                settle(pe)
                with pe.Fori(0, slabs_n // RING) as g:
                    for j in range(RING):
                        pe.wait_ge(lo_ready, layer * SLABS + at0 + g * RING + j + 1)
                        pe.wait_ge(evac, layer * ev_per_layer + ev_at + g * RING + j + 1)
                        slab_product(j, act_hi, act_lo)

            def group(layer, at0, ev_at, hi=act_hi, lo=act_lo):
                for j in range(RING):
                    pe.wait_ge(lo_ready, layer * SLABS + at0 + j + 1)
                    pe.wait_ge(act_evac, layer * ACT_EVS + ev_at + j + 1)
                    slab_product(j, hi, lo)

            def mean_square(sq_count):
                pe.wait_ge(sq_ready, sq_count)
                for k in range(KB):
                    last = nc.tensor.matmul(ps[:, 7, 0:T], ones[:], sq[:, k, :], start=(k == 0), stop=(k == KB - 1))
                last.then_inc(ms_ready, 1)

            def x_group(layer, at0, ev_at):
                def chunk(k):
                    pe.wait_ge(sq_chunk, layer * CHUNKED + ev_at + k + 1)
                    return nc.tensor.matmul(ps[:, 7, 0:T], ones[:], sq[:, k, :], start=(k == 0), stop=(k == KB - 1))

                for n in range(KB):
                    pe.wait_ge(lo_ready, layer * SLABS + at0 + n + 1)
                    pe.wait_ge(dve_evac, layer * DVE_EVS + ev_at + n + 1)
                    slab_product(n % RING, act_hi, act_lo)
                    if n:
                        chunk(n - 1)
                chunk(KB - 1).then_inc(ms_ready, 1)

            def operand(layer, use):
                pe.wait_ge(act_ready, layer * (2 * USES) + 2 * use + 2)

            nc.tensor.sem_inc(gate_mm, RING)
            pe.wait_ge(consts, 4)
            with pe.Fori(0, DEPTH) as layer:
                mean_square(layer * WHOLE + 1)
                operand(layer, USE_MIX)
                pe.wait_ge(wif_ready, layer + 1)
                for b in range(TB):
                    for k in range(KB):
                        for i, (a, w) in enumerate(((act_hi, wif_hi), (act_lo, wif_hi), (act_hi, wif_lo))):
                            last = nc.tensor.matmul(ps[:, 4, 8 * b:8 * b + 8], a[:, k, b * P:(b + 1) * P], w[:, k, :],
                                                    start=(k == 0 and i == 0), stop=(k == KB - 1 and i == 2))
                last.then_inc(gates_mm, 1)
                group(layer, Z_Q, Z_Q)
                mean_square(layer * WHOLE + 2)
                pe.wait_ge(ls_ready, layer + 1)
                nc.tensor.matmul(ps[:, 6, 0:4], tri[:], ls[:, 0, :], start=True, stop=True)
                nc.tensor.matmul(ps[:, 6, 4:8], tri[:], ls[:, 1, :], start=True, stop=False)
                nc.tensor.matmul(ps[:, 6, 4:8], ones[:], ls[:, 0, :], start=False, stop=True).then_inc(cum_ready, 1)
                group(layer, Z_K, Z_K)
                pe.wait_ge(r_ready, layer + 1)
                for i, src in enumerate((r_nat, b_nat)):
                    for b in range(TB):
                        last = nc.tensor.transpose(ps[0:4, 5, i * T + b * P:i * T + (b + 1) * P], src[:, b, :], ident[:])
                last.then_inc(rows_mm, 1)
                group(layer, Z_V, Z_V)
                pe.wait_ge(root_ready, layer * NORMS + NORM_MEM + 1)
                pe.wait_ge(e_ready, layer + 1)
                for bank, row in ((6, m_row), (4, e_row)):
                    for h in range(LH):
                        last = nc.tensor.matmul(pair(bank, 4)[:, h, :], ident[0:4, h:h + 1].to_broadcast([4, P]), row[:],
                                                start=True, stop=True)
                last.then_inc(bc_mm, 1)
                group(layer, Z_O, Z_O)
                pe.wait_ge(e_bc_ready, layer + 1)
                for b in range(TB):
                    for h in range(LH):
                        last = nc.tensor.transpose(ps[:, 4 + b, h * P:(h + 1) * P], zT[:, Z_V + h, b * P:(b + 1) * P], ident[:])
                last.then_inc(v_tr, 1)
                group(layer, Z_B, Z_B)
                pe.wait_ge(arg_ready, layer + 1)
                pe.wait_ge(v_nat_ready, layer + 1)
                for h in range(LH):
                    nc.tensor.matmul(ps[:, 4 + h, 0:T], zT[:, Z_K + h, 0:P], zT[:, Z_Q + h, :], start=True, stop=True)
                    last = nc.tensor.matmul(ps[:, 4 + h, T:384], zT[:, Z_K + h, P:T], zT[:, Z_Q + h, P:T],
                                            start=True, stop=True)
                last.then_inc(qk_mm, 1)
                group(layer, Z_U, Z_U)
                pe.wait_ge(s_ready, layer + 1)
                for h in range(LH):
                    for bank, lhs in ((4, None), (6, ones)):
                        o = pair(bank, 4)[:, h, :]
                        nc.tensor.matmul(o, v_nat[:, 0, h, :] if lhs is None else lhs[:], s_w[:, h, 0:T],
                                         start=True, stop=False)
                        last = nc.tensor.matmul(o[:, P:T], v_nat[:, 1, h, :] if lhs is None else lhs[:], s_w[:, h, T:384],
                                                start=False, stop=True)
                last.then_inc(nd_mm, 1)
                group(layer, Z_C, Z_C)
                pe.wait_ge(hsq_ready, layer + 1)
                for i in range(2):
                    last = nc.tensor.matmul(ps[:, 6 + i, :], ones[:], den[:, 2 * i:2 * i + 2, :].rearrange("p i t -> p (i t)"),
                                            start=True, stop=True)
                last.then_inc(hms_mm, 1)
                pe.wait_ge(act_ready, layer * (2 * USES) + 2 * USE_MEM + 2)
                group(layer, K1_AT, K_EV, mem_hi, mem_lo)
                operand(layer, USE_Y)
                pe.wait_ge(act_evac, layer * ACT_EVS + K_EV + 4 + RING)
                x_group(layer, OUT_AT, 0)
                pe.wait_ge(dve_evac, layer * DVE_EVS + OUT_SLABS + RING)
                group(layer, K2_AT, K_EV + 4, mem_hi, mem_lo)
                operand(layer, USE_XATTN)
                project(layer, Q_AT, Q_SLABS, act_evac, Q_EV, ACT_EVS)
                pe.wait_ge(act_evac, layer * ACT_EVS + PQ_EV + RING)
                for b in range(TB):
                    for h in range(XH):
                        for c in range(2):
                            last = nc.tensor.matmul(pair(4, 8)[:, b * XH + h, :], qT[:, 2 * h + c, b * P:(b + 1) * P],
                                                    kT[:, 2 * h + c, :], start=(c == 0), stop=(c == 1))
                last.then_inc(xs_mm, 1)

                def memory_values(n):
                    pe.wait_ge(lo_ready, layer * SLABS + XV_AT + n + 1)
                    for b in range(2):
                        for half in range(2):
                            for i, (w, a) in enumerate(((w_hi, mem_hi), (w_lo, mem_hi), (w_hi, mem_lo))):
                                last = nc.tensor.matmul(ps[:, 2 * b + half, :], a[:, n, b * P:(b + 1) * P],
                                                        w[:, n % RING, 4 * half:4 * half + 4, :].rearrange("p k c -> p (k c)"),
                                                        start=(n == 0 and i == 0), stop=(n == KB - 1 and i == 2))
                    last.then_inc(slab_done, 1)

                for n in range(4):
                    memory_values(n)
                pe.wait_ge(prob_ready, layer + 1)
                for mb in range(2):
                    for h in range(XH):
                        for b in range(TB):
                            last = nc.tensor.transpose(pair(4 + 2 * mb, 4)[:, h, b * P:(b + 1) * P],
                                                       prob[:, b * XH + h, mb * P:(mb + 1) * P], ident[:])
                last.then_inc(pt_mm, 1)
                for n in range(4, KB):
                    memory_values(n)
                pe.wait_ge(vmem_dve, layer + 1)
                pe.wait_ge(vmem_act, layer + 1)
                pe.wait_ge(pt_dve, layer + 1)
                pe.wait_ge(pt_act, layer + 1)
                for half in range(2):
                    for c in range(4 * half, 4 * half + 4):
                        for mb in range(2):
                            last = nc.tensor.matmul(pair(4, 8)[:, c, :], v_mem[:, mb, c * P:(c + 1) * P],
                                                    probT[:, mb, c // 2, :], start=(mb == 0), stop=(mb == 1))
                    last.then_inc(xo_mm, 1)
                operand(layer, USE_AO)
                x_group(layer, XO_AT, OUT_SLABS)
                operand(layer, USE_FFN)
                project(layer, PQ_AT, PQ_SLABS, act_evac, PQ_EV, ACT_EVS)
                pe.wait_ge(act_evac, layer * ACT_EVS + U_EV + RING)
                pe.wait_ge(keys_loaded, layer * 16 + 16)

                def scores(b):
                    for n in range(SETS):
                        last = nc.tensor.matmul(ps[:, 4 + n // 4, (n % 4) * P:(n % 4 + 1) * P],
                                                qpT[:, n, b * P:(b + 1) * P], skT[:, n, :], start=True, stop=True)
                    last.then_inc(sc_mm, 1)

                scores(0)
                project(layer, U_AT, RING, act_evac, U_EV, ACT_EVS)
                pe.wait_ge(sc_evac, layer * TB + 1)
                scores(1)
                project(layer, U_AT + RING, RETRIEVED - RING, act_evac, U_EV + RING, ACT_EVS)
                pe.wait_ge(decoded, layer + 1)
                for i, src in enumerate((row_f[:], col_f[:], g_exp[:].rearrange("p c k -> p (c k)"))):
                    for b in range(TB):
                        last = nc.tensor.transpose(ps[:, 4 + i // 2, (i % 2) * T + b * P:(i % 2) * T + (b + 1) * P],
                                                   src[:, b * P:(b + 1) * P], ident[:])
                last.then_inc(ret_mm, 1)
                project(layer, U_AT + RETRIEVED, U_SLABS - RETRIEVED, act_evac, U_EV + RETRIEVED, ACT_EVS)

                with pe.Fori(0, GROUPS // RING) as g:
                    for s in range(RING):
                        n = g * RING + s
                        pe.wait_ge(hot_col_ready, layer * GROUPS + n + 1)
                        pe.wait_ge(hot_row_ready, layer * GROUPS + n + 1)
                        pe.wait_ge(hot_act_ready, layer * GROUPS + n + 1)
                        for i in range(4):
                            last = nc.tensor.matmul(ps[:, 4 + s, i * P:(i + 1) * P], hot_col[:, s, i, :],
                                                    hot_row[:, s, i, :], start=True, stop=True)
                        last.then_inc(gate_mm, 1)

                def expert_out(n, j, first=False, final=False):
                    pe.wait_ge(lo_ready, layer * SLABS + V_AT + n + 1)
                    pe.wait_ge(ga_ready, layer * V_SLABS + n + 1)
                    for b in range(TB):
                        for half in range(2):
                            for i, (w, a) in enumerate(PARTS):
                                last = nc.tensor.matmul(ps[:, 2 * b + half, :], a[:, j, b * P:(b + 1) * P],
                                                        w[:, j, 4 * half:4 * half + 4, :].rearrange("p k c -> p (k c)"),
                                                        start=(first and i == 0), stop=(final and i == 2))
                    last.then_inc(slab_done, 1)

                pe.wait_ge(act_evac, (layer + 1) * ACT_EVS + RING)
                for j in range(RING):
                    expert_out(j, j, first=(j == 0))
                with pe.Fori(1, V_SLABS // RING - 1) as g:
                    for j in range(RING):
                        expert_out(g * RING + j, j)
                for j in range(RING):
                    expert_out(V_SLABS - RING + j, j, final=(j == RING - 1))
                for b in range(TB):
                    for half in range(2):
                        pe.wait_ge((y_ready, y_act_ready)[b], layer * 2 + half + 1)
                        for c in range(4):
                            last = nc.tensor.transpose(pair(4, 8)[:, 4 * half + c, b * P:(b + 1) * P],
                                                       y_nat[:, 2 * b + half, c * P:(c + 1) * P], ident[:])
                last.then_inc(y_mm, 1)
            mean_square(DEPTH * WHOLE + 1)



def kernel(x, mem, g_mix, w_in, b_if, conv_w, conv_b, g_head, w_out, g_xattn, g_mem,
           w_xq, w_xk, w_xv, w_xo, g_ffn, w_pq, sub_keys, u_experts, v_experts, g_final):
    import numpy as np
    import concourse.bacc as bacc
    from concourse.bass_utils import run_bass_kernel_spmd

    def col(a):
        return np.asarray(a).reshape(DEPTH, -1, P).transpose(0, 2, 1)

    def slab(w):
        w = np.asarray(w)
        return w.reshape(DEPTH, KB, P, -1, P).transpose(0, 3, 2, 1, 4).reshape(DEPTH, -1, P, D)

    w_in = np.asarray(w_in)
    cols = IN_SLABS * P
    z, k = slab(w_in[:, :, :cols]), slab(w_xk)
    parts = [z[:, at:at + 4] for at in Z_ORDER]
    parts += [k[:, 0:4], slab(w_out), k[:, 4:8], slab(w_xq), np.asarray(w_xv).reshape(DEPTH, KB, P, D),
              slab(w_xo), slab(w_pq),
             np.asarray(u_experts).reshape(DEPTH, NKEYS, NKEYS, KB, P).transpose(0, 1, 4, 3, 2).reshape(DEPTH, NKEYS, P, D),
             np.asarray(v_experts).reshape(DEPTH, NKEYS, P, D)]
    slabs = np.concatenate(parts, axis=1).reshape(DEPTH * SLABS, P, D)
    w_if = w_in[:, :, cols:].reshape(DEPTH, KB, P, 8).transpose(0, 2, 1, 3).reshape(DEPTH, P, KB * 8)
    cw = np.asarray(conv_w)
    params = np.concatenate([col(g_mix), col(g_mem), col(g_xattn), col(g_ffn), col(g_head),
                             col(cw.reshape(DEPTH, -1)), col(conv_b),
                             np.broadcast_to(np.asarray(b_if)[:, None, :], (DEPTH, P, 8)), w_if], axis=2)
    arrays = {
        "x": np.asarray(x)[0].reshape(T, KB, P).transpose(2, 1, 0),
        "mem": np.asarray(mem)[0].reshape(NMEM, KB, P).transpose(2, 1, 0),
        "slabs": slabs,
        "params": params,
        "g_final": np.asarray(g_final).reshape(KB, P).transpose(1, 0),
        "sub_keys": np.asarray(sub_keys).reshape(DEPTH, SETS, NKEYS, P).transpose(0, 3, 1, 2),
    }
    arrays = {name: np.ascontiguousarray(a) for name, a in arrays.items()}
    nc = bacc.Bacc("TRN2", target_bir_lowering=False, num_devices=1)
    args = [nc.dram_tensor(name, a.shape, FP32, kind="ExternalInput").ap() for name, a in arrays.items()]
    out = nc.dram_tensor("out", (P, KB, T), FP32, kind="ExternalOutput").ap()
    trunk(nc, *args, out)
    got = run_bass_kernel_spmd(nc, [arrays], core_ids=[0]).results[0]["out"]
    return got.transpose(2, 1, 0).reshape(1, T, D)
```

```python
from contextlib import ExitStack

import concourse.bass as bass
from concourse import mybir

FP32 = mybir.dt.float32
F32R = mybir.dt.float32r
U32 = mybir.dt.uint32
ALU = mybir.AluOpType
ACT = mybir.ActivationFunctionType
AX = mybir.AxisListType
ds = bass.ds

P = 128
D = 1024
KB = D // P
T = 256
TB = T // P
NMEM = 256
DEPTH = 2
EPS = 1e-6
LH = 4
LSTM_SCALE = 128 ** -0.5
XH = 4
X_SCALE = 256 ** -0.5
PH = 8
SETS = 2 * PH
TOPK = 16
NKEYS = 128
LOWEST = -3.4028234663852886e38

IN_SLABS, K_SLABS, OUT_SLABS, Q_SLABS, XV_SLABS, XO_SLABS, PQ_SLABS = 28, 8, 8, 8, 8, 8, 16
U_SLABS = V_SLABS = 128
IN_AT = 0
K1_AT = IN_AT + IN_SLABS
OUT_AT = K1_AT + K_SLABS // 2
K2_AT = OUT_AT + OUT_SLABS
Q_AT = K2_AT + K_SLABS // 2
XV_AT = Q_AT + Q_SLABS
XO_AT = XV_AT + XV_SLABS
PQ_AT = XO_AT + XO_SLABS
U_AT = PQ_AT + PQ_SLABS
V_AT = U_AT + U_SLABS
SLABS = V_AT + V_SLABS
Z_Q, Z_K, Z_V, Z_O, Z_B, Z_U, Z_C = range(0, IN_SLABS, 4)
Z_ORDER = (12, 16, 20, 24, 0, 8, 4)
RING = 4
IN_EV, K_EV = 0, IN_SLABS
Q_EV = K_EV + K_SLABS
PQ_EV = Q_EV + Q_SLABS
U_EV = PQ_EV + PQ_SLABS
ACT_EVS = U_EV + U_SLABS
DVE_EVS = OUT_SLABS + XO_SLABS

G_MIX, G_MEM, G_XATTN, G_FFN = 0, 8, 16, 24
G_HEAD, CONV_W, CONV_B, B_IF, W_IF = 32, 36, 48, 52, 60
N_PARAM = W_IF + KB * 8

USE_MIX, USE_MEM, USE_Y, USE_XATTN, USE_AO, USE_FFN, USES = range(7)
XN_INDEX = {USE_MIX: 0, USE_MEM: 1, USE_Y: 2, USE_XATTN: 3, USE_FFN: 4}
XN_USES = len(XN_INDEX)
PRE_MIX, PRE_FFN = 0, 1
X_PARTS = 4
SUM_MIX, SUM_MEM, SUM_OUT, SUM_XO, SUMS = 0, 3, 6, 12, 18
CHUNKED = 2 * KB
NORM_MIX, NORM_MEM, NORM_XATTN, NORM_FFN, NORMS = range(5)
WHOLE = 2

KEYS_READ = 64
RETRIEVED = 88
ACT_SLOTS, POOL_SLOTS = (0, 2), (1, 3)
GROUPS = T // 4


class Steps:

    def __init__(self, eng, sem):
        self.eng, self.sem, self.n = eng, sem, 0

    def mark(self, ins):
        ins.then_inc(self.sem, 1)
        self.n += 1

    def join(self):
        self.eng.wait_ge(self.sem, self.n)

    def link(self, ins):
        self.mark(ins)
        self.join()

    def restart(self):
        self.join()
        self.eng.sem_clear(self.sem)
        self.n = 0


def trunk(nc, x, mem, slabs, params, sub_keys, out):
    ctx = ExitStack()
    with ctx:
        base = (nc.sbuf_base + 63) // 64 * 64
        limit = nc.sbuf_usable_end
        ctx.enter_context(nc.sbuf_tensor("arena", [P, (limit - base - 64) // 4], FP32))
        top = [base]

        def at(name, offset, shape, dt=FP32):
            return nc.alloc_sbuf_tensor_at(name, shape, dt, offset=offset)

        def sb(name, shape, dt=FP32):
            size = 4
            for n in shape[1:]:
                size *= n
            t = at(name, top[0], shape, dt)
            top[0] += (size + 31) // 32 * 32
            assert top[0] <= limit, name
            return t

        raw = sb("raw", [P, RING, D])
        w_hi = sb("w_hi", [P, RING, KB, P], F32R)
        w_lo = sb("w_lo", [P, RING, KB, P], F32R)
        xT = sb("xT", [P, KB, T])
        act_at = top[0]
        act_hi = sb("act_hi", [P, KB, T], F32R)
        act_lo = sb("act_lo", [P, KB, T], F32R)
        hot_col = at("hot_col", act_at, [P, RING, 4, P])
        y_nat = [at(f"y_nat{b}", act_at + (2 * b + 1) * RING * T * 4, [P, 2, 512]) for b in range(TB)]
        hot_row = at("hot_row", act_at + RING * 4 * P * 4, [P, RING, 4, P])
        ident = sb("ident", [P, P])
        eps = sb("eps", [P, 1])
        ones = sb("ones", [P, P])
        tri = sb("tri", [P, P])
        iota = sb("iota", [P, P])
        par = sb("par", [P, N_PARAM])
        wif_hi = sb("wif_hi", [P, KB, 8], F32R)
        wif_lo = sb("wif_lo", [P, KB, 8], F32R)
        rowT = sb("rowT", [P, T])
        colT = sb("colT", [P, T])
        gateT = sb("gateT", [P, T])
        ngateT = sb("ngateT", [P, T])
        cols16 = sb("cols16", [P, 4 * RING])
        gated_at = top[0]
        gated = sb("gated", [P, NKEYS, T])

        def tmp(name, kib, shape, dt=FP32):
            size = 4
            for n in shape[1:]:
                size *= n
            assert kib * 1024 + size <= NKEYS * T * 4, name
            return at(name, gated_at + int(kib * 1024), shape, dt)

        memT = tmp("memT", 0, [P, KB, NMEM])
        mem_lo = tmp("mem_lo", 0, [P, KB, NMEM], F32R)
        mem_hi = tmp("mem_hi", 120, [P, KB, NMEM], F32R)
        kT = tmp("kT", 8, [P, K_SLABS, NMEM])
        v_mem = tmp("v_mem", 24, [P, 2, D])
        zT = tmp("zT", 32, [P, IN_SLABS, T])
        u_pad = tmp("u_pad", 60, [P, 4, T + 2])
        conv = tmp("conv", 65, [P, 4, T])
        v_nat = tmp("v_nat", 69, [P, TB, LH, P])
        arg = tmp("arg", 73, [P, LH, 384])
        s_w = tmp("s_w", 79, [P, LH, 384])
        hsq = tmp("hsq", 85, [P, LH, T])
        hl = tmp("hl", 89, [P, LH, T])
        o_sig = tmp("o_sig", 93, [P, LH, T])
        gates = tmp("gates", 97, [P, TB, 8])
        nf = tmp("nf", 97.25, [P, TB, 4])
        ef = tmp("ef", 97.5, [P, TB, 4])
        ls = tmp("ls", 97.75, [P, TB, 4])
        b_nat = tmp("b_nat", 98, [P, TB, 4])
        r_nat = tmp("r_nat", 98.25, [P, TB, 4])
        mf = tmp("mf", 98.5, [P, TB, 4])
        d2 = tmp("d2", 103, [P, 2, TB, 4])
        hroot = tmp("hroot", 103.25, [P, TB, 4])
        r_row = tmp("r_row", 99, [4, T])
        m_row = tmp("m_row", 100, [4, T])
        e_row = tmp("e_row", 101, [4, T])
        rstd = tmp("rstd", 102, [P, T])
        rstd_pre = tmp("rstd_pre", 16, [P, T])
        sq_sum = tmp("sq_sum", 17, [P, T])
        g_row = tmp("g_row", 18, [8, T])
        pre_hi = tmp("pre_hi", 80, [P, KB, T], F32R)
        pre_lo = tmp("pre_lo", 88, [P, KB, T], F32R)
        sq = tmp("sq", 104, [P, KB, T])
        xn = tmp("xn", 112, [P, KB, T])
        skT = tmp("skT", 120, [P, SETS, NKEYS])
        qT = tmp("qT", 32, [P, KB, T])
        prob = tmp("prob", 40, [P, 2 * XH, NMEM])
        probT = tmp("probT", 48, [P, 2, XH, T])
        rmax = tmp("rmax", 97, [P, 8])
        nmax = tmp("nmax", 97.25, [P, 8])
        rsum = tmp("rsum", 97.5, [P, 8])
        rinv = tmp("rinv", 97.75, [P, 8])
        qpT = tmp("qpT", 64, [P, SETS, T])
        scores1 = tmp("scores1", 64, [P, SETS, NKEYS])
        scores0 = tmp("scores0", 80, [P, SETS, NKEYS])
        top_v = tmp("top_v", RETRIEVED, [P, TB * SETS, TOPK])
        top_i = tmp("top_i", 90, [P, TB * SETS, TOPK])
        fin_v = tmp("fin_v", 92, [P, TB * PH, TOPK])
        fin_i = tmp("fin_i", 93, [P, TB * PH, TOPK], U32)
        a_u = tmp("a_u", 94, [P, TB * PH * TOPK], U32)
        b_u = tmp("b_u", 95, [P, TB * PH * TOPK], U32)
        a_f = tmp("a_f", 96, [P, TB * PH * TOPK])
        b_f = tmp("b_f", 97, [P, TB * PH * TOPK])
        row_f = tmp("row_f", 98, [P, TB * PH * TOPK])
        col_f = tmp("col_f", 99, [P, TB * PH * TOPK])
        g_exp = tmp("g_exp", 100, [P, TB * PH, TOPK])
        g_sum = tmp("g_sum", 101, [P, TB * PH])
        pick = tmp("pick", 104, [P, TB * PH * TOPK, TOPK])
        top_u = tmp("top_u", 104, [P, TB * SETS, TOPK], U32)
        cand = tmp("cand", 106, [P, 2, TOPK * TOPK])
        struck = tmp("struck", 108, [P, 2, TOPK * TOPK])

        ps = ctx.enter_context(nc.psum_tensor("ps", [P, 8, 512], FP32))

        def pair(b0, n):
            return ps[:, b0:b0 + n // 2, :].rearrange("p b (i t) -> p (b i) t", i=2)

        def sem(name):
            return ctx.enter_context(nc.semaphore(name))

        raw_loaded = [sem(f"raw_loaded{j}") for j in range(RING)]
        hi_ready, lo_ready, slab_done = sem("hi_ready"), sem("lo_ready"), sem("slab_done")
        act_evac, dve_evac = sem("act_evac"), sem("dve_evac")
        x_loaded, x_ffn, par_loaded = sem("x_loaded"), sem("x_ffn"), sem("par_loaded")
        mem_loaded, keys_loaded, out_stored = sem("mem_loaded"), sem("keys_loaded"), sem("out_stored")
        consts, const_step, pool_step = sem("consts"), sem("const_step"), sem("pool_step")
        sq_ready, ms_ready, xn_ready = sem("sq_ready"), sem("ms_ready"), sem("xn_ready")
        root_ready, hroot_ready, d2_ready = sem("root_ready"), sem("hroot_ready"), sem("d2_ready")
        act_hi_ready, act_ready = sem("act_hi_ready"), sem("act_ready")
        wif_hi_ready, wif_ready, gates_mm = sem("wif_hi_ready"), sem("wif_ready"), sem("gates_mm")
        g_row_ready, gates_tr = sem("g_row_ready"), sem("gates_tr")
        nf_ready, lnf_ready, ls_ready = sem("nf_ready"), sem("lnf_ready"), sem("ls_ready")
        cum_ready, r_ready, rows_mm = sem("cum_ready"), sem("r_ready"), sem("rows_mm")
        eb_ready, e_ready, bc_mm, pre_hi_ready = sem("eb_ready"), sem("e_ready"), sem("bc_mm"), sem("pre_hi_ready")
        pre_ready, scaled, y_done, summed = sem("pre_ready"), sem("scaled"), sem("y_done"), sem("summed")
        v2_ready, diag_ready, hr_mm = sem("v2_ready"), sem("diag_ready"), sem("hr_mm")
        v_tr, v_nat_ready = sem("v_tr"), sem("v_nat_ready")
        vmem_mm, vmem_act, vmem_dve, sq_chunk = sem("vmem_mm"), sem("vmem_act"), sem("vmem_dve"), sem("sq_chunk")
        o_ready, qk_mm, arg_ready, dw_ready = sem("o_ready"), sem("qk_mm"), sem("arg_ready"), sem("dw_ready")
        s_ready, nd_mm, hl_ready, hsq_ready, hms_mm = (sem("s_ready"), sem("nd_mm"), sem("hl_ready"),
                                                      sem("hsq_ready"), sem("hms_mm"))
        xs_mm, nmax_ready, exp_ready, prob_ready = sem("xs_mm"), sem("nmax_ready"), sem("exp_ready"), sem("prob_ready")
        pt_mm, pt_dve, pt_act, xo_mm = sem("pt_mm"), sem("pt_dve"), sem("pt_act"), sem("xo_mm")
        sc_mm, sc_evac, fin_ready, gexp_ready = sem("sc_mm"), sem("sc_evac"), sem("fin_ready"), sem("gexp_ready")
        keys_read, decoded, ret_mm, cols_ready = sem("keys_read"), sem("decoded"), sem("ret_mm"), sem("cols_ready")
        hot_act_ready, y_ready, y_act_ready, y_mm = sem("hot_act_ready"), sem("y_ready"), sem("y_act_ready"), sem("y_mm")
        hot_col_ready, hot_row_ready, gate_mm = sem("hot_col_ready"), sem("hot_row_ready"), sem("gate_mm")
        gated_ready, ga_hi_ready, ga_ready = sem("gated_ready"), sem("ga_hi_ready"), sem("ga_ready")
        settled = sem("settled")
        act_step, dve_step, out_ready = sem("act_step"), sem("dve_step"), sem("out_ready")

        def settle(eng):
            eng.sem_inc(settled, 1)

        block = ctx.enter_context(nc.Block())

        @block.sync
        def _(sp):
            def load(j, slab):
                sp.dma_start(raw[:, j, :], slab).then_inc(raw_loaded[j], 16)

            sp.dma_start(xT[:], x).then_inc(x_loaded, 16)
            for j in range(RING):
                load(j, slabs[j])
            with sp.Fori(1, DEPTH * SLABS // RING) as g:
                for j in range(RING):
                    sp.wait_ge(lo_ready, g * RING + (j - RING + 1))
                    load(j, slabs[ds(g * RING + j, 1)].rearrange("o p f -> (o p) f"))
            for j in range(RING):
                sp.wait_ge(lo_ready, DEPTH * SLABS - RING + j + 1)
                load(j, slabs[j])
            for half in range(2):
                sp.wait_ge(out_ready, half + 1)
                sp.dma_start(out[:, 4 * half:4 * half + 4, :], xn[:, 4 * half:4 * half + 4, :]).then_inc(out_stored, 16)
            sp.wait_ge(out_stored, 32)

        @block.gpsimd
        def _(pool):
            nc.gpsimd.memset(ident[:], 0.0).then_inc(const_step, 1)
            nc.gpsimd.memset(ones[:], 1.0).then_inc(const_step, 1)
            nc.gpsimd.memset(eps[:], EPS).then_inc(consts, 1)
            pool.wait_ge(const_step, 2)
            nc.gpsimd.affine_select(out=ident[:], in_=ident[:], compare_op=ALU.not_equal, fill=1.0,
                                    base=0, pattern=[[-1, P]], channel_multiplier=1).then_inc(consts, 1)
            nc.gpsimd.affine_select(out=tri[:], in_=ones[:], compare_op=ALU.is_ge, fill=0.0,
                                    base=0, pattern=[[1, P]], channel_multiplier=-1).then_inc(consts, 1)
            nc.gpsimd.iota(iota[:], [[1, P]], base=0, channel_multiplier=0,
                           allow_small_or_imprecise_dtypes=True).then_inc(consts, 1)
            pool.dma_start(par[:], params[0]).then_inc(par_loaded, 16)

            def scale(dst, count, evacs, xns):
                pool.wait_ge(xn_ready, xns)
                pool.wait_ge(act_evac, evacs)
                for i in range(count):
                    last = nc.gpsimd.tensor_tensor(dst[:, i, :], dst[:, i, :], rstd_pre[:], ALU.mult)
                last.then_inc(scaled, 1)

            def sum_halves(layer, at0, squares):
                pool.wait_ge(sq_ready, layer * WHOLE + squares)
                for i, n in enumerate((4, 2, 1)):
                    if i:
                        pool.wait_ge(summed, layer * SUMS + at0 + i)
                    dst = sq_sum[:].unsqueeze(1) if n == 1 else sq[:, 0:n, :]
                    nc.gpsimd.tensor_tensor(dst, sq[:, 0:n, :], sq[:, n:2 * n, :], ALU.add).then_inc(summed, 1)

            def sum_chunks(layer, at0, chunks):
                for n in range(1, KB - 1):
                    pool.wait_ge(sq_chunk, layer * CHUNKED + chunks + n + 1)
                    if n > 1:
                        pool.wait_ge(summed, layer * SUMS + at0 + n - 1)
                    nc.gpsimd.tensor_tensor(sq_sum[:], sq[:, 0, :] if n == 1 else sq_sum[:], sq[:, n, :],
                                            ALU.add).then_inc(summed, 1)

            with pool.Fori(0, DEPTH) as layer:
                pool.wait_ge(x_ffn, layer * X_PARTS + X_PARTS)
                settle(pool)
                pool.dma_start(memT[:], mem).then_inc(mem_loaded, 16)
                sum_halves(layer, SUM_MIX, 1)
                sum_halves(layer, SUM_MEM, 2)
                scale(zT, 2 * RING, layer * ACT_EVS + 2 * RING + RING, layer * (2 * XN_USES) + 2 * XN_INDEX[USE_MIX] + 1)
                sum_chunks(layer, SUM_OUT, 0)
                pool.wait_ge(slab_done, layer * SLABS + XO_AT)
                pool.dma_start(skT[:], sub_keys[ds(layer, 1)].rearrange("o p s k -> (o p) s k")).then_inc(keys_loaded, 16)
                sum_chunks(layer, SUM_XO, OUT_SLABS)
                scale(qpT, 2 * RING, layer * ACT_EVS + PQ_EV + 2 * RING + RING, layer * (2 * XN_USES) + 2 * XN_INDEX[USE_FFN] + 1)
                pool.wait_ge(act_ready, (layer + 1) * (2 * USES))
                settle(pool)
                pool.dma_start(par[:], params[ds(layer + 1, 1)].rearrange("o p f -> (o p) f")).then_inc(par_loaded, 16)
                pool.wait_ge(cols_ready, layer + 1)
                pool.wait_ge(slab_done, layer * SLABS + V_AT)
                settle(pool)
                with pool.Fori(0, GROUPS // RING) as g:
                    nc.gpsimd.tensor_copy(cols16[:], colT[:, ds(g * (4 * RING), 4 * RING)]).then_inc(pool_step, 1)
                    pool.wait_ge(pool_step, layer * (GROUPS // RING) + g + 1)
                    for s in POOL_SLOTS:
                        pool.wait_ge(gate_mm, layer * GROUPS + g * RING + s + 1)
                        settle(pool)
                        for i in range(4):
                            last = nc.gpsimd.tensor_scalar(hot_col[:, s, i, :], iota[:],
                                                           cols16[:, 4 * s + i:4 * s + i + 1], None, ALU.is_equal)
                        last.then_inc(hot_col_ready, 1)
                    pool.wait_ge(hot_col_ready, layer * (GROUPS // 2) + g * 2 + 2)

        @block.scalar
        def _(act):
            step = Steps(act, act_step)

            def turn(layer, at0, g, j, evac):
                act.wait_ge(slab_done, layer * SLABS + at0 + g * RING + j + 1)
                if evac is not None:
                    evac(j, g * RING + j).then_inc(act_evac, 1)
                act.wait_ge(raw_loaded[j], (layer * (SLABS // RING) + (at0 // RING + 2) + g) * 16)
                nc.scalar.activation(w_hi[:, j].rearrange("p k c -> p (k c)"), raw[:, j, :],
                                     ACT.Copy).then_inc(hi_ready, 1)

            def group(layer, at0, evac=None, slots=range(RING)):
                for j in slots:
                    turn(layer, at0, 0, j, evac)

            def section(layer, at0, slabs_n, evac=None):
                with act.Fori(0, slabs_n // RING) as g:
                    for j in range(RING):
                        turn(layer, at0, g, j, evac)

            def copy_to(dst, first=0):
                return lambda j, n: nc.scalar.activation(dst[:, ds(n + first, 1), :], ps[:, j:j + 1, 0:T], ACT.Copy)

            def squares(src):
                nc.scalar.activation(sq[:], src[:], ACT.Square, scale=D ** -0.5).then_inc(sq_ready, 1)

            def roots(count, dst=rstd, bank=7):
                act.wait_ge(ms_ready, count)
                nc.scalar.activation(dst[:], ps[:, bank, 0:T], ACT.Sqrt, bias=eps[:]).then_inc(root_ready, 1)

            def pre_part(k, g_col):
                nc.scalar.activation(pre_hi[:, k, :], xT[:, k, :], ACT.Copy,
                                     scale=par[:, g_col + k:g_col + k + 1]).then_inc(pre_hi_ready, 1)

            def x_group(layer, at0, ev, pre=None):
                for n in range(KB):
                    if n < KB - 1:
                        turn(layer, at0 + n // RING * RING, 0, n % RING, None)
                    act.wait_ge(dve_evac, layer * DVE_EVS + ev + RING + n + 1)
                    if pre is not None:
                        pre_part(n, pre)
                    nc.scalar.activation(sq[:, n, :], xT[:, n, :], ACT.Square, scale=D ** -0.5).then_inc(sq_chunk, 1)
                turn(layer, at0 + RING, 0, RING - 1, None)

            def operand_hi(layer, use, free_at=None, dst=act_hi, order=(0, 1)):
                if free_at is not None:
                    act.wait_ge(slab_done, layer * SLABS + free_at)
                for i, half in enumerate(order):
                    act.wait_ge(xn_ready, layer * (2 * XN_USES) + 2 * XN_INDEX[use] + i + 1)
                    nc.scalar.activation(dst[:, 4 * half:4 * half + 4], xn[:, 4 * half:4 * half + 4],
                                         ACT.Copy).then_inc(act_hi_ready, 1)

            act.wait_ge(consts, 4)
            nc.scalar.sem_inc(act_evac, RING)
            for j in range(RING):
                act.wait_ge(raw_loaded[j], 16)
                nc.scalar.activation(w_hi[:, j].rearrange("p k c -> p (k c)"), raw[:, j, :],
                                     ACT.Copy).then_inc(hi_ready, 1)
            with act.Fori(0, DEPTH) as layer:
                act.wait_ge(par_loaded, layer * 16 + 16)
                for k in range(KB):
                    if k % 2 == 0:
                        act.wait_ge(x_ffn, layer * X_PARTS + k // 2 + 1)
                    pre_part(k, G_MIX)
                squares(xT)
                nc.scalar.activation(wif_hi[:].rearrange("p k c -> p (k c)"), par[:, W_IF:W_IF + KB * 8],
                                     ACT.Copy).then_inc(wif_hi_ready, 1)
                group(layer, Z_Q, copy_to(zT, Z_Q), (0, 1))
                roots(layer * NORMS + NORM_MIX + 1, rstd_pre)
                group(layer, Z_Q, copy_to(zT, Z_Q), (2, 3))
                operand_hi(layer, USE_MIX)
                group(layer, Z_K, copy_to(zT, Z_K), (0, 1))
                act.wait_ge(nf_ready, layer + 1)
                step.link(nc.scalar.activation(ef[:], nf[:], ACT.Exp))
                nc.scalar.activation(ef[:], ef[:], ACT.Ln, bias=1.0).then_inc(lnf_ready, 1)
                step.restart()
                act.wait_ge(mem_loaded, layer * 16 + 16)
                squares(memT)
                group(layer, Z_K, copy_to(zT, Z_K), (2, 3))
                group(layer, Z_V, copy_to(zT, Z_V), (0, 1))
                roots(layer * NORMS + NORM_MEM + 1)
                group(layer, Z_V, copy_to(zT, Z_V), (2, 3))
                operand_hi(layer, USE_MEM, dst=mem_hi)
                act.wait_ge(eb_ready, layer + 1)
                nc.scalar.activation(e_row[:], e_row[:], ACT.Exp, scale=-1.0).then_inc(e_ready, 1)
                group(layer, Z_O, copy_to(zT, Z_O), (0, 1))
                act.wait_ge(arg_ready, layer + 1)
                nc.scalar.activation(arg[:], arg[:], ACT.Exp, scale=-1.0).then_inc(dw_ready, 1)
                group(layer, Z_O, copy_to(zT, Z_O), (2, 3))
                act.wait_ge(v_tr, layer + 1)
                nc.scalar.activation(v_nat[:].rearrange("p b h c -> p (b h c)"),
                                     ps[:, 4:6, :].rearrange("p b c -> p (b c)"), ACT.Copy).then_inc(v_nat_ready, 1)
                act.wait_ge(act_evac, layer * ACT_EVS + Z_O + 4 + RING)
                nc.scalar.activation(o_sig[:], zT[:, Z_O:Z_O + 4, :], ACT.Sigmoid).then_inc(o_ready, 1)
                group(layer, Z_B, copy_to(zT, Z_B))
                group(layer, Z_U, copy_to(zT, Z_U))
                act.wait_ge(nd_mm, layer + 1)
                nc.scalar.activation(d2[:].rearrange("p i b h -> p (i b h)"), ps[:, 6, 0:16], ACT.Square,
                                     scale=EPS ** 0.5).then_inc(d2_ready, 1)
                act.wait_ge(hl_ready, layer + 1)
                nc.scalar.activation(hsq[:], hl[:], ACT.Square).then_inc(hsq_ready, 1)
                group(layer, Z_C, copy_to(zT, Z_C), (0, 1))
                act.wait_ge(v2_ready, layer + 1)
                nc.scalar.activation(hroot[:], d2[:, 0], ACT.Sqrt).then_inc(hroot_ready, 1)
                group(layer, Z_C, copy_to(zT, Z_C), (2, 3))
                group(layer, K1_AT, copy_to(kT), (0, 1))
                operand_hi(layer, USE_Y, K1_AT, order=(1, 0))
                group(layer, K1_AT, copy_to(kT), (2, 3))
                x_group(layer, OUT_AT, 0)
                roots(layer * NORMS + NORM_XATTN + 1)
                operand_hi(layer, USE_XATTN, K2_AT)
                group(layer, K2_AT, copy_to(kT, 4))
                section(layer, Q_AT, Q_SLABS, copy_to(qT))
                for b in range(TB):
                    act.wait_ge(nmax_ready, layer * TB + b + 1)
                    for i in range(b * XH, (b + 1) * XH):
                        last = nc.scalar.activation(prob[:, i, :], pair(4, 8)[:, i, :], ACT.Exp, bias=nmax[:, i:i + 1],
                                                    scale=X_SCALE, accum_out=rsum[:, i:i + 1])
                    last.then_inc(exp_ready, 1)
                group(layer, XV_AT)
                act.wait_ge(pt_mm, layer + 1)
                nc.scalar.activation(probT[:, 1], pair(6, 4), ACT.Copy).then_inc(pt_act, 1)
                group(layer, XV_AT + RING, slots=(0, 1, 2))
                for half in range(2):
                    act.wait_ge(*((vmem_mm, layer + 1), (slab_done, layer * SLABS + XO_AT))[half])
                    nc.scalar.activation(v_mem[:, 1, half * 512:half * 512 + 512], ps[:, 2 + half, :],
                                         ACT.Copy).then_inc(vmem_act, 1)
                group(layer, XV_AT + RING, slots=(3,))
                for half in range(2):
                    act.wait_ge(xo_mm, layer * 2 + half + 1)
                    nc.scalar.activation(act_hi[:, 4 * half:4 * half + 4], pair(4 + 2 * half, 4),
                                         ACT.Copy).then_inc(act_hi_ready, 1)
                x_group(layer, XO_AT, OUT_SLABS, G_FFN)
                roots(layer * NORMS + NORM_FFN + 1, rstd_pre)
                group(layer, PQ_AT, copy_to(qpT))
                operand_hi(layer, USE_FFN, PQ_AT)
                section(layer, PQ_AT + RING, PQ_SLABS - RING, copy_to(qpT, RING))

                def gelu_to(first):
                    return lambda j, n: nc.scalar.activation(gated[:, ds(n + first, 1), :], ps[:, j:j + 1, 0:T], ACT.Gelu)

                def scores_out(b, dst):
                    act.wait_ge(sc_mm, layer * TB + b + 1)
                    nc.scalar.activation(dst[:].rearrange("p n k -> p (n k)"),
                                         ps[:, 4:8, :].rearrange("p b c -> p (b c)"), ACT.Copy).then_inc(sc_evac, 1)

                scores_out(0, scores0)
                section(layer, U_AT, RING, gelu_to(0))
                scores_out(1, scores1)
                section(layer, U_AT + RING, KEYS_READ - RING, gelu_to(RING))
                act.wait_ge(keys_read, layer + 1)
                section(layer, U_AT + KEYS_READ, RING, gelu_to(KEYS_READ))
                act.wait_ge(fin_ready, layer + 1)
                nc.scalar.activation(g_exp[:], g_exp[:], ACT.Exp).then_inc(gexp_ready, 1)
                section(layer, U_AT + KEYS_READ + RING, RETRIEVED - KEYS_READ - RING, gelu_to(KEYS_READ + RING))
                act.wait_ge(ret_mm, layer + 1)
                section(layer, U_AT + RETRIEVED, U_SLABS - RETRIEVED, gelu_to(RETRIEVED))

                def gated_hi(j, n):
                    nc.scalar.activation(act_hi[:, j:j + 1, :], gated[:, n, :], ACT.Copy).then_inc(ga_hi_ready, 1)

                act.wait_ge(cols_ready, layer + 1)
                settle(act)
                with act.Fori(0, GROUPS // RING) as g:
                    for s in ACT_SLOTS:
                        act.wait_ge(gate_mm, layer * GROUPS + g * RING + s + 1)
                        settle(act)
                        tokens = [ds(g * (4 * RING) + 4 * s + i, 1) for i in range(4)]
                        for i, token in enumerate(tokens):
                            last = nc.scalar.activation(hot_col[:, s, i, :], iota[:], ACT.Abs, scale=-1.0,
                                                        bias=colT[:, token])
                        step.link(last)
                        for i, token in enumerate(tokens):
                            last = nc.scalar.activation(hot_col[:, s, i, :], hot_col[:, s, i, :], ACT.Relu,
                                                        scale=ngateT[:, token], bias=gateT[:, token])
                        last.then_inc(hot_act_ready, 1)
                    step.restart()
                act.wait_ge(gated_ready, layer + 1)
                for j in range(RING):
                    gated_hi(j, slice(j, j + 1))
                with act.Fori(0, V_SLABS // RING - 1) as g:
                    for j in range(RING):
                        act.wait_ge(slab_done, layer * SLABS + V_AT + g * RING + j + 1)
                        act.wait_ge(raw_loaded[j], (layer * (SLABS // RING) + (V_AT // RING + 2) + g) * 16)
                        nc.scalar.activation(w_hi[:, j].rearrange("p k c -> p (k c)"), raw[:, j, :],
                                             ACT.Copy).then_inc(hi_ready, 1)
                        gated_hi(j, ds(g * RING + RING + j, 1))

                def next_layers(j):
                    act.wait_ge(slab_done, layer * SLABS + SLABS - RING + j + 1)
                    act.wait_ge(raw_loaded[j], (layer + 1) * (SLABS // RING * 16) + 16)
                    nc.scalar.activation(w_hi[:, j].rearrange("p k c -> p (k c)"), raw[:, j, :],
                                         ACT.Copy).then_inc(hi_ready, 1)

                for j in range(RING - 1):
                    next_layers(j)
                act.wait_ge(y_done, layer * 3 + 2)
                nc.scalar.activation(y_nat[1][:, 0, :], ps[:, 2, :], ACT.Copy).then_inc(y_act_ready, 1)
                act.wait_ge(slab_done, layer * SLABS + SLABS)
                nc.scalar.activation(y_nat[1][:, 1, :], ps[:, 3, :], ACT.Copy).then_inc(y_act_ready, 1)
                next_layers(RING - 1)
            for k in range(KB):
                if k % 2 == 0:
                    act.wait_ge(x_ffn, DEPTH * X_PARTS + k // 2 + 1)
                nc.scalar.activation(sq[:, k, :], xT[:, k, :], ACT.Square, scale=D ** -0.5).then_inc(sq_chunk, 1)
            roots(DEPTH * NORMS + 1, bank=0)

        @block.vector
        def _(dve):
            step = Steps(dve, dve_step)

            def lo_part(layer, at0, g, j):
                dve.wait_ge(hi_ready, layer * SLABS + at0 + g * RING + j + 1)
                nc.vector.tensor_tensor(w_lo[:, j].rearrange("p k c -> p (k c)"), raw[:, j, :],
                                        w_hi[:, j].rearrange("p k c -> p (k c)").bitcast(FP32),
                                        ALU.subtract).then_inc(lo_ready, 1)

            def group(layer, at0, slots=range(RING)):
                for j in slots:
                    lo_part(layer, at0 + RING, 0, j)

            def pre_rest(layer, use, k, g_col):
                dve.wait_ge(pre_hi_ready, layer * (2 * KB) + use * KB + k + 1)
                nc.vector.scalar_tensor_tensor(pre_lo[:, k, :], xT[:, k, :], par[:, g_col + k:g_col + k + 1],
                                               pre_hi[:, k, :].bitcast(FP32), ALU.mult, ALU.subtract).then_inc(pre_ready, 1)

            def x_group(layer, at0, pre=None):
                for n in range(KB):
                    dve.wait_ge(slab_done, layer * SLABS + at0 + n + 1)
                    add_to_x(n % RING, n).then_inc(dve_evac, 1)
                    if n < KB - 1:
                        lo_part(layer, at0 + RING + n // RING * RING, 0, n % RING)
                    if pre is not None:
                        pre_rest(layer, PRE_FFN, n, pre)
                lo_part(layer, at0 + 2 * RING, 0, RING - 1)

            def section(layer, at0, slabs_n):
                with dve.Fori(0, slabs_n // RING) as g:
                    for j in range(RING):
                        lo_part(layer, at0 + RING, g, j)

            def add_to_x(j, n):
                return nc.vector.tensor_tensor(xT[:, ds(n, 1), :], xT[:, ds(n, 1), :], ps[:, j:j + 1, 0:T], ALU.add)

            def norm(src, g_col, norm_count, half_done, rstd=rstd):
                dve.wait_ge(root_ready, norm_count)
                step.link(nc.vector.reciprocal(rstd[:], rstd[:]))
                for half in range(2):
                    for k in range(4 * half, 4 * half + 4):
                        last = nc.vector.scalar_tensor_tensor(xn[:, k, :], src[:, k, :], g_col[:, k:k + 1], rstd[:],
                                                              ALU.mult, ALU.mult)
                    half_done(last)

            def operand_lo(layer, use, hi=act_hi, lo=act_lo, order=(0, 1)):
                for i, half in enumerate(order):
                    h = slice(4 * half, 4 * half + 4)
                    dve.wait_ge(act_hi_ready, layer * (2 * USES) + 2 * use + i + 1)
                    nc.vector.tensor_tensor(lo[:, h], pair(4 + 2 * half, 4) if use == USE_AO else xn[:, h],
                                            hi[:, h].bitcast(FP32), ALU.subtract).then_inc(act_ready, 1)

            def to_xn(ins):
                ins.then_inc(xn_ready, 1)

            nc.vector.sem_inc(dve_evac, RING)
            dve.wait_ge(x_loaded, 16)
            nc.vector.sem_inc(x_ffn, X_PARTS)
            for j in range(RING):
                dve.wait_ge(hi_ready, j + 1)
                nc.vector.tensor_tensor(w_lo[:, j].rearrange("p k c -> p (k c)"), raw[:, j, :],
                                        w_hi[:, j].rearrange("p k c -> p (k c)").bitcast(FP32),
                                        ALU.subtract).then_inc(lo_ready, 1)
            dve.wait_ge(consts, 4)
            with dve.Fori(0, DEPTH) as layer:
                dve.wait_ge(par_loaded, layer * 16 + 16)
                for k in range(KB):
                    pre_rest(layer, PRE_MIX, k, G_MIX)
                dve.wait_ge(wif_hi_ready, layer + 1)
                nc.vector.tensor_tensor(wif_lo[:].rearrange("p k c -> p (k c)"), par[:, W_IF:W_IF + KB * 8],
                                        wif_hi[:].rearrange("p k c -> p (k c)").bitcast(FP32),
                                        ALU.subtract).then_inc(wif_ready, 1)
                group(layer, Z_Q, (0, 1))
                norm(xT, par[:, G_MIX:G_MIX + 8], layer * NORMS + NORM_MIX + 1, to_xn, rstd_pre)
                operand_lo(layer, USE_MIX)
                group(layer, Z_Q, (2, 3))
                dve.wait_ge(gates_mm, layer + 1)
                nc.vector.tensor_copy(g_row[:], ps[0:8, 4, 0:T]).then_inc(g_row_ready, 1)
                group(layer, Z_K, (0, 1))
                dve.wait_ge(gates_tr, layer + 1)
                step.link(nc.vector.tensor_tensor(
                    gates[:], ps[:, 4, 0:16].rearrange("p (b c) -> p b c", b=TB),
                    par[:, B_IF:B_IF + 8].unsqueeze(1).to_broadcast([P, TB, 8]), ALU.add))
                nc.vector.scalar_tensor_tensor(nf[:], gates[:, :, 4:8], -1.0, gates[:, :, 4:8], ALU.mult, ALU.min).then_inc(nf_ready, 1)
                step.mark(nc.vector.tensor_scalar(mf[:], gates[:, :, 4:8], 0.0, None, ALU.min))
                dve.wait_ge(lnf_ready, layer + 1)
                step.join()
                nc.vector.tensor_tensor(ls[:], mf[:], ef[:], ALU.subtract).then_inc(ls_ready, 1)
                group(layer, Z_K, (2, 3))
                dve.wait_ge(cum_ready, layer + 1)
                step.link(nc.vector.tensor_copy(b_nat[:], ps[:, 6, 0:8].rearrange("p (b h) -> p b h", b=TB)))
                nc.vector.tensor_tensor(r_nat[:], gates[:, :, 0:4], b_nat[:], ALU.subtract).then_inc(r_ready, 1)
                group(layer, Z_V, (0, 1))
                norm(memT, par[:, G_MEM:G_MEM + 8], layer * NORMS + NORM_MEM + 1, to_xn)
                group(layer, Z_V, (2, 3))
                dve.wait_ge(rows_mm, layer + 1)
                step.link(nc.vector.tensor_copy(r_row[:], ps[0:4, 5, 0:T]))
                step.link(nc.vector.tensor_tensor_scan(m_row[:], r_row[:], r_row[:], 0.0, ALU.max, ALU.max))
                nc.vector.tensor_tensor(e_row[:], m_row[:], ps[0:4, 5, T:2 * T], ALU.add).then_inc(eb_ready, 1)
                operand_lo(layer, USE_MEM, mem_hi, mem_lo)
                group(layer, Z_O, (0, 1))
                dve.wait_ge(bc_mm, layer + 1)
                for h in range(LH):
                    m_bc = pair(6, 4)[:, h, :]
                    nc.vector.tensor_scalar(arg[:, h, 0:T], m_bc, r_nat[:, 0, h:h + 1], 0.0, ALU.subtract, ALU.max)
                    last = nc.vector.tensor_scalar(arg[:, h, T:384], m_bc[:, P:T], r_nat[:, 1, h:h + 1], 0.0,
                                                   ALU.subtract, ALU.max)
                last.then_inc(arg_ready, 1)
                group(layer, Z_O, (2, 3))
                dve.wait_ge(dw_ready, layer + 1)
                diag = arg[:].rearrange("p h (i t) -> p h i t", i=3)[:, :, 0:3:2, :]
                step.link(nc.vector.tensor_tensor(diag, diag, tri[:].unsqueeze(1).unsqueeze(1).to_broadcast([P, LH, 2, P]),
                                                  ALU.mult))
                nc.vector.memset(u_pad[:, :, 0:2], 0.0)
                group(layer, Z_B)
                dve.wait_ge(qk_mm, layer + 1)
                for h in range(LH):
                    last = nc.vector.scalar_tensor_tensor(s_w[:, h, :], ps[:, 4 + h, 0:384], LSTM_SCALE, arg[:, h, :],
                                                          ALU.mult, ALU.mult)
                last.then_inc(s_ready, 1)
                group(layer, Z_U)
                dve.wait_ge(nd_mm, layer + 1)
                dve.wait_ge(o_ready, layer + 1)
                nc.vector.tensor_tensor(hl[:], pair(4, 4), o_sig[:], ALU.mult).then_inc(hl_ready, 1)
                dve.wait_ge(d2_ready, layer + 1)
                step.mark(nc.vector.scalar_tensor_tensor(d2[:, 0], d2[:, 0], 1e-30, d2[:, 1], ALU.max, ALU.max))
                dve.wait_ge(act_evac, layer * ACT_EVS + Z_U + 4 + RING)
                step.link(nc.vector.tensor_tensor(u_pad[:, :, 2:T + 2], zT[:, Z_U:Z_U + 4, :], zT[:, Z_B:Z_B + 4, :], ALU.mult))
                group(layer, Z_C, (0, 1))
                dve.wait_ge(hms_mm, layer + 1)
                nc.vector.scalar_tensor_tensor(d2[:, 0], ps[:, 7, 0:8].rearrange("p (b h) -> p b h", b=TB), 1.0 / P, d2[:, 0],
                                               ALU.mult, ALU.add).then_inc(v2_ready, 1)
                for m in range(4):
                    last = nc.vector.tensor_scalar(conv[:, m, :], u_pad[:, m, 2:T + 2],
                                                   par[:, CONV_W + 8 + m:CONV_W + 9 + m], par[:, CONV_B + m:CONV_B + m + 1],
                                                   ALU.mult, ALU.add)
                step.mark(last)
                dve.wait_ge(hroot_ready, layer + 1)
                step.link(nc.vector.reciprocal(hroot[:], hroot[:]))
                nc.vector.tensor_tensor(hsq[:].rearrange("p h (b t) -> p h b t", b=TB),
                                        ident[:].unsqueeze(1).unsqueeze(1).to_broadcast([P, LH, TB, P]),
                                        hroot[:].rearrange("p b h -> p h b").unsqueeze(3).to_broadcast([P, LH, TB, P]),
                                        ALU.mult).then_inc(diag_ready, 1)
                for tap in (1, 0):
                    for m in range(4):
                        last = nc.vector.scalar_tensor_tensor(conv[:, m, :], u_pad[:, m, tap:tap + T],
                                                              par[:, CONV_W + 4 * tap + m:CONV_W + 4 * tap + m + 1],
                                                              conv[:, m, :], ALU.mult, ALU.add)
                    step.link(last)
                group(layer, Z_C, (2, 3))
                dve.wait_ge(hr_mm, layer + 1)
                for h in range(LH):
                    last = nc.vector.scalar_tensor_tensor(xn[:, 4 + h, :], hl[:, h, :], par[:, G_HEAD + h:G_HEAD + h + 1],
                                                          pair(6, 4)[:, h, :], ALU.mult, ALU.mult)
                last.then_inc(xn_ready, 1)
                dve.wait_ge(act_evac, layer * ACT_EVS + K_EV + RING)
                nc.vector.tensor_tensor(xn[:, 0:4, :], conv[:], zT[:, Z_C:Z_C + 4, :], ALU.mult).then_inc(xn_ready, 1)
                group(layer, K1_AT, (0, 1))
                operand_lo(layer, USE_Y, order=(1, 0))
                group(layer, K1_AT, (2, 3))
                x_group(layer, OUT_AT)
                norm(xT, par[:, G_XATTN:G_XATTN + 8], layer * NORMS + NORM_XATTN + 1, to_xn)
                operand_lo(layer, USE_XATTN)
                group(layer, K2_AT)
                section(layer, Q_AT, Q_SLABS)
                blocks = [slice(b * XH, (b + 1) * XH) for b in range(TB)]
                for b, h in enumerate(blocks):
                    dve.wait_ge(xs_mm, layer * TB + b + 1)
                    step.link(nc.vector.tensor_reduce(rmax[:, h], pair(4, 8)[:, h], AX.X, ALU.max))
                    nc.vector.tensor_scalar(nmax[:, h], rmax[:, h], -X_SCALE, None, ALU.mult).then_inc(nmax_ready, 1)
                for b, h in enumerate(blocks):
                    dve.wait_ge(exp_ready, layer * TB + b + 1)
                    step.link(nc.vector.reciprocal(rinv[:, h], rsum[:, h]))
                    nc.vector.tensor_tensor(prob[:, h], prob[:, h], rinv[:, h].unsqueeze(2).to_broadcast([P, XH, NMEM]),
                                            ALU.mult).then_inc(prob_ready, 1)
                group(layer, XV_AT)
                dve.wait_ge(pt_mm, layer + 1)
                nc.vector.tensor_copy(probT[:, 0], pair(4, 4)).then_inc(pt_dve, 1)
                group(layer, XV_AT + RING, (0, 1, 2))
                for half in range(2):
                    dve.wait_ge(*((vmem_mm, layer + 1), (slab_done, layer * SLABS + XO_AT))[half])
                    nc.vector.tensor_copy(v_mem[:, 0, half * 512:half * 512 + 512], ps[:, half, :]).then_inc(vmem_dve, 1)
                group(layer, XV_AT + RING, (3,))
                operand_lo(layer, USE_AO)
                x_group(layer, XO_AT, G_FFN)
                norm(xT, par[:, G_FFN:G_FFN + 8], layer * NORMS + NORM_FFN + 1, to_xn, rstd_pre)
                group(layer, PQ_AT)
                operand_lo(layer, USE_FFN)
                section(layer, PQ_AT + RING, PQ_SLABS - RING)

                def slab(i):
                    lo_part(layer, U_AT + i - i % RING, 0, i % RING)

                def top16(first, second, beside):
                    rows = (first, second)
                    for src, _, v, _ in rows:
                        step.mark(nc.vector.max(v[:, 0:8], src))
                    slab(beside)
                    step.join()
                    for src, struck, v, i in rows:
                        nc.vector.max_index(i[:, 0:8], v[:, 0:8], src)
                        step.mark(nc.vector.match_replace(struck, v[:, 0:8], src, LOWEST))
                    slab(beside + 1)
                    step.join()
                    for _, struck, v, _ in rows:
                        step.mark(nc.vector.max(v[:, 8:16], struck))
                    step.join()
                    for _, struck, v, i in rows:
                        step.mark(nc.vector.max_index(i[:, 8:16], v[:, 8:16], struck))

                for n in range(0, TB * SETS, 2):
                    if n % SETS == 0:
                        dve.wait_ge(sc_evac, layer * TB + n // SETS + 1)
                        settle(dve)
                    src = (scores0, scores1)[n // SETS]
                    step.join()
                    top16(*[(src[:, m % SETS, :], struck[:, m - n, 0:NKEYS], top_v[:, m, :], top_u[:, m, :])
                            for m in (n, n + 1)], beside=n + RING)
                step.join()
                nc.vector.tensor_copy(top_i[:], top_u[:]).then_inc(keys_read, 1)
                for n in range(0, TB * PH, 2):
                    step.join()
                    for m in (n, n + 1):
                        step.mark(nc.vector.tensor_tensor(
                            cand[:, m - n, :].rearrange("p (a b) -> p a b", a=TOPK),
                            top_v[:, 2 * m, :].unsqueeze(2).to_broadcast([P, TOPK, TOPK]),
                            top_v[:, 2 * m + 1, :].unsqueeze(1).to_broadcast([P, TOPK, TOPK]), ALU.add))
                    slab(RING + TB * SETS + 2 * n)
                    step.join()
                    top16(*[(cand[:, m - n, :], struck[:, m - n, :], fin_v[:, m, :], fin_i[:, m, :])
                            for m in (n, n + 1)], beside=RING + TB * SETS + 2 * n + 1)
                    slab(RING + TB * SETS + 2 * n + 3)
                step.join()
                at_slab = RING + TB * SETS + 2 * TB * PH
                nc.vector.tensor_tensor(g_exp[:], fin_v[:], fin_v[:, :, 0:1].to_broadcast([P, TB * PH, TOPK]),
                                        ALU.subtract).then_inc(fin_ready, 1)
                flat_i = fin_i[:].rearrange("p c k -> p (c k)")
                step.mark(nc.vector.tensor_scalar(a_u[:], flat_i, 4, None, ALU.logical_shift_right))
                step.mark(nc.vector.tensor_scalar(b_u[:], flat_i, 15, None, ALU.bitwise_and))
                slab(at_slab)
                step.join()
                step.mark(nc.vector.tensor_copy(a_f[:], a_u[:]))
                step.mark(nc.vector.tensor_copy(b_f[:], b_u[:]))
                slab(at_slab + 1)
                keys = top_i[:].rearrange("p (c s) a -> p c s a", s=2)
                pick4 = pick[:].rearrange("p (c k) a -> p c k a", k=TOPK)
                n = at_slab + 2
                for side, (place, found) in enumerate(((a_f, row_f), (b_f, col_f))):
                    step.join()
                    step.mark(nc.vector.tensor_tensor(
                        pick[:], place[:].unsqueeze(2).to_broadcast([P, TB * PH * TOPK, TOPK]),
                        iota[:, 0:TOPK].unsqueeze(1).to_broadcast([P, TB * PH * TOPK, TOPK]), ALU.is_equal))
                    for i in range(3):
                        slab(n + i)
                    step.join()
                    step.mark(nc.vector.tensor_tensor(
                        pick4, pick4, keys[:, :, side, :].unsqueeze(2).to_broadcast([P, TB * PH, TOPK, TOPK]), ALU.mult))
                    for i in range(3, 6):
                        slab(n + i)
                    step.join()
                    step.mark(nc.vector.tensor_reduce(found[:], pick[:], AX.X, ALU.add))
                    for i in range(6, 8):
                        slab(n + i)
                    n += 8
                step.join()
                dve.wait_ge(gexp_ready, layer + 1)
                step.mark(nc.vector.tensor_reduce(g_sum[:], g_exp[:], AX.X, ALU.add))
                slab(n)
                step.join()
                step.mark(nc.vector.reciprocal(g_sum[:], g_sum[:]))
                slab(n + 1)
                step.join()
                nc.vector.tensor_tensor(g_exp[:], g_exp[:], g_sum[:].unsqueeze(2).to_broadcast([P, TB * PH, TOPK]),
                                        ALU.mult).then_inc(decoded, 1)
                assert n + 2 == RETRIEVED, n
                section(layer, U_AT + RETRIEVED - RING, RING)
                dve.wait_ge(ret_mm, layer + 1)
                step.mark(nc.vector.tensor_copy(rowT[:], ps[:, 4, 0:T]))
                step.mark(nc.vector.tensor_copy(gateT[:], ps[:, 5, 0:T]))
                step.mark(nc.vector.tensor_scalar(ngateT[:], ps[:, 5, 0:T], -1.0, None, ALU.mult))
                nc.vector.tensor_copy(colT[:], ps[:, 4, T:2 * T]).then_inc(cols_ready, 1)
                section(layer, U_AT + RETRIEVED, U_SLABS - RETRIEVED)
                step.join()

                def hot(n, s):
                    dve.wait_ge(gate_mm, layer * GROUPS + n + 1)
                    if s in ACT_SLOTS:
                        last = nc.vector.tensor_tensor(hot_row[:, s], iota[:].unsqueeze(1).to_broadcast([P, 4, P]),
                                                       rowT[:, ds(n * 4, 4)].unsqueeze(2).to_broadcast([P, 4, P]),
                                                       ALU.is_equal)
                    else:
                        for i in range(4):
                            t = n * 4 + i
                            last = nc.vector.tensor_scalar(hot_row[:, s, i, :], iota[:], rowT[:, ds(t, 1)],
                                                           gateT[:, ds(t, 1)], ALU.is_equal, ALU.mult)
                    last.then_inc(hot_row_ready, 1)

                def gate(n, s, final=False):
                    dve.wait_ge(gate_mm, layer * GROUPS + n + 1 + RING)
                    g4 = gated[:, :, ds(n * 4, 4)].rearrange("p i t -> p t i")
                    return nc.vector.tensor_tensor(g4, g4, ps[:, 4 + s, :].rearrange("p (t i) -> p t i", t=4), ALU.mult)

                dve.wait_ge(slab_done, layer * SLABS + V_AT)
                hot(0, 0)
                hot(1, 1)
                dve.wait_ge(act_evac, (layer + 1) * ACT_EVS + RING)
                settle(dve)
                with dve.Fori(0, GROUPS // RING - 1) as g:
                    for s in range(RING):
                        hot(g * RING + s + 2, (s + 2) % RING)
                        gate(g * RING + s, s)
                hot(GROUPS - 2, 2)
                gate(GROUPS - 4, 0)
                hot(GROUPS - 1, 3)
                for s in (1, 2, 3):
                    last = gate(GROUPS - 4 + s, s)
                last.then_inc(gated_ready, 1)

                def gated_lo(j, n, ready):
                    dve.wait_ge(ga_hi_ready, ready)
                    nc.vector.tensor_tensor(act_lo[:, j:j + 1, :], gated[:, n, :], act_hi[:, j:j + 1, :].bitcast(FP32),
                                            ALU.subtract).then_inc(ga_ready, 1)

                for j in range(RING):
                    gated_lo(j, slice(j, j + 1), layer * V_SLABS + j + 1)
                with dve.Fori(0, V_SLABS // RING - 1) as g:
                    for j in range(RING):
                        lo_part(layer, V_AT + RING, g, j)
                        gated_lo(j, ds(g * RING + RING + j, 1), layer * V_SLABS + g * RING + RING + j + 1)
                for j in range(RING - 1):
                    lo_part(layer, SLABS, 0, j)
                for half in range(2):
                    dve.wait_ge(y_done, layer * 3 + 2 * half + 1)
                    nc.vector.tensor_copy(y_nat[0][:, half, :], ps[:, half, :]).then_inc(y_ready, 1)
                for m in range(X_PARTS):
                    dve.wait_ge(y_mm, layer * 2 + m // 2 + 1)
                    nc.vector.tensor_tensor(xT[:, 2 * m:2 * m + 2, :], xT[:, 2 * m:2 * m + 2, :],
                                            pair(4, 8)[:, 2 * m:2 * m + 2, :], ALU.add).then_inc(x_ffn, 1)
                lo_part(layer, SLABS, 0, RING - 1)
                step.restart()
            dve.wait_ge(par_loaded, DEPTH * 16 + 16)
            norm(xT, par[:, G_MIX:G_MIX + 8], DEPTH * NORMS + 1, lambda ins: ins.then_inc(out_ready, 1))

        @block.tensor
        def _(pe):
            PARTS = ((w_hi, act_hi), (w_lo, act_hi), (w_hi, act_lo))

            def slab_product(j, hi, lo, before=None):
                for k in range(KB):
                    if before is not None:
                        before(k)
                    for i, (w, a) in enumerate(((w_hi, hi), (w_lo, hi), (w_hi, lo))):
                        last = nc.tensor.matmul(ps[:, j, 0:T], w[:, j, k, :], a[:, k, :],
                                                start=(k == 0 and i == 0), stop=(k == KB - 1 and i == 2))
                last.then_inc(slab_done, 1)

            def project(layer, at0, slabs_n, evac, ev_at, ev_per_layer):
                settle(pe)
                with pe.Fori(0, slabs_n // RING) as g:
                    for j in range(RING):
                        pe.wait_ge(lo_ready, layer * SLABS + at0 + g * RING + j + 1)
                        pe.wait_ge(evac, layer * ev_per_layer + ev_at + g * RING + j + 1)
                        slab_product(j, act_hi, act_lo)

            def group(layer, at0, ev_at, hi=act_hi, lo=act_lo, slots=range(RING), before=None):
                for j in slots:
                    pe.wait_ge(lo_ready, layer * SLABS + at0 + j + 1)
                    pe.wait_ge(act_evac, layer * ACT_EVS + ev_at + j + 1)
                    slab_product(j, hi, lo, before if j == 0 else None)

            def mean_square(layer, at0):
                pe.wait_ge(summed, layer * SUMS + at0 + 3)
                nc.tensor.matmul(ps[:, 7, 0:T], ones[:], sq_sum[:], start=True, stop=True).then_inc(ms_ready, 1)

            def x_mean_square(layer, at0, ev_at):
                pe.wait_ge(summed, layer * SUMS + at0 + 6)
                nc.tensor.matmul(ps[:, 7, 0:T], ones[:], sq_sum[:], start=True, stop=False)
                pe.wait_ge(sq_chunk, layer * CHUNKED + ev_at + KB)
                nc.tensor.matmul(ps[:, 7, 0:T], ones[:], sq[:, KB - 1, :], start=False, stop=True).then_inc(ms_ready, 1)

            def x_group(layer, at0, ev_at, before=None):
                for n in range(KB):
                    pe.wait_ge(lo_ready, layer * SLABS + at0 + n + 1)
                    pe.wait_ge(dve_evac, layer * DVE_EVS + ev_at + n + 1)
                    slab_product(n % RING, act_hi, act_lo, before if n == 0 else None)

            def operand(layer, use):
                pe.wait_ge(act_ready, layer * (2 * USES) + 2 * use + 2)

            nc.tensor.sem_inc(gate_mm, RING)
            pe.wait_ge(consts, 4)
            with pe.Fori(0, DEPTH) as layer:
                def pre_chunk(k):
                    pe.wait_ge(pre_ready, layer * (2 * KB) + PRE_MIX * KB + k + 1)

                group(layer, Z_Q, Z_Q, pre_hi, pre_lo, (0, 1), pre_chunk)
                mean_square(layer, SUM_MIX)
                group(layer, Z_Q, Z_Q, pre_hi, pre_lo, (2, 3))
                group(layer, Z_K, Z_K, pre_hi, pre_lo, (0, 1))
                operand(layer, USE_MIX)
                pe.wait_ge(wif_ready, layer + 1)
                for k in range(KB):
                    for i, (w, a) in enumerate(((wif_hi, act_hi), (wif_lo, act_hi), (wif_hi, act_lo))):
                        last = nc.tensor.matmul(ps[0:8, 4, 0:T], w[:, k, :], a[:, k, :],
                                                start=(k == 0 and i == 0), stop=(k == KB - 1 and i == 2))
                last.then_inc(gates_mm, 1)
                group(layer, Z_K, Z_K, pre_hi, pre_lo, (2,))
                pe.wait_ge(g_row_ready, layer + 1)
                settle(pe)
                for b in range(TB):
                    last = nc.tensor.transpose(ps[:, 4, 8 * b:8 * b + 8], g_row[:, b * P:(b + 1) * P], ident[0:8, 0:8])
                last.then_inc(gates_tr, 1)
                group(layer, Z_K, Z_K, pre_hi, pre_lo, (3,))
                group(layer, Z_V, Z_V, slots=(0, 1))
                pe.wait_ge(ls_ready, layer + 1)
                nc.tensor.matmul(ps[:, 6, 0:4], tri[:], ls[:, 0, :], start=True, stop=True)
                nc.tensor.matmul(ps[:, 6, 4:8], tri[:], ls[:, 1, :], start=True, stop=False)
                nc.tensor.matmul(ps[:, 6, 4:8], ones[:], ls[:, 0, :], start=False, stop=True).then_inc(cum_ready, 1)
                mean_square(layer, SUM_MEM)
                group(layer, Z_V, Z_V, slots=(2, 3))
                pe.wait_ge(r_ready, layer + 1)
                for i, src in enumerate((r_nat, b_nat)):
                    for b in range(TB):
                        last = nc.tensor.transpose(ps[0:4, 5, i * T + b * P:i * T + (b + 1) * P], src[:, b, :], ident[:])
                last.then_inc(rows_mm, 1)
                group(layer, Z_O, Z_O, slots=(0, 1))
                pe.wait_ge(root_ready, layer * NORMS + NORM_MEM + 1)
                pe.wait_ge(eb_ready, layer + 1)
                for h in range(LH):
                    last = nc.tensor.matmul(pair(6, 4)[:, h, :], ident[0:4, h:h + 1].to_broadcast([4, P]), m_row[:],
                                            start=True, stop=True)
                last.then_inc(bc_mm, 1)
                group(layer, Z_O, Z_O, slots=(2, 3))
                for b in range(TB):
                    for h in range(LH):
                        last = nc.tensor.transpose(ps[:, 4 + b, h * P:(h + 1) * P], zT[:, Z_V + h, b * P:(b + 1) * P], ident[:])
                last.then_inc(v_tr, 1)
                group(layer, Z_B, Z_B)
                pe.wait_ge(arg_ready, layer + 1)
                pe.wait_ge(v_nat_ready, layer + 1)
                pe.wait_ge(scaled, layer * 2 + 1)
                for h in range(LH):
                    nc.tensor.matmul(ps[:, 4 + h, 0:T], zT[:, Z_K + h, 0:P], zT[:, Z_Q + h, :], start=True, stop=True)
                    last = nc.tensor.matmul(ps[:, 4 + h, T:384], zT[:, Z_K + h, P:T], zT[:, Z_Q + h, P:T],
                                            start=True, stop=True)
                last.then_inc(qk_mm, 1)
                group(layer, Z_U, Z_U)
                pe.wait_ge(s_ready, layer + 1)
                pe.wait_ge(e_ready, layer + 1)
                for h in range(LH):
                    o = pair(4, 4)[:, h, :]
                    nc.tensor.matmul(o, v_nat[:, 0, h, :], s_w[:, h, 0:T], start=True, stop=False)
                    nc.tensor.matmul(o[:, P:T], v_nat[:, 1, h, :], s_w[:, h, T:384], start=False, stop=True)
                for h in range(LH):
                    nc.tensor.matmul(ps[:, 6, h:h + 1], s_w[:, h, 0:P], ones[:, 0:1], start=True, stop=True)
                    nc.tensor.matmul(ps[:, 6, LH + h:LH + h + 1], s_w[:, h, P:T], ones[:, 0:1], start=True, stop=False)
                    nc.tensor.matmul(ps[:, 6, LH + h:LH + h + 1], s_w[:, h, T:384], ones[:, 0:1],
                                     start=False, stop=True)
                for b in range(TB):
                    last = nc.tensor.transpose(ps[:, 6, 8 + 4 * b:12 + 4 * b], e_row[:, b * P:(b + 1) * P], ident[0:4, 0:4])
                last.then_inc(nd_mm, 1)
                group(layer, Z_C, Z_C, slots=(0, 1))
                pe.wait_ge(hsq_ready, layer + 1)
                for b in range(TB):
                    for h in range(LH):
                        last = nc.tensor.matmul(ps[:, 7, LH * b + h:LH * b + h + 1], hsq[:, h, b * P:(b + 1) * P],
                                                ones[:, 0:1], start=True, stop=True)
                last.then_inc(hms_mm, 1)
                group(layer, Z_C, Z_C, slots=(2, 3))
                pe.wait_ge(diag_ready, layer + 1)
                for i in range(2):
                    last = nc.tensor.matmul(ps[:, 6 + i, :], ones[:], hsq[:, 2 * i:2 * i + 2, :].rearrange("p i t -> p (i t)"),
                                            start=True, stop=True)
                last.then_inc(hr_mm, 1)
                pe.wait_ge(act_ready, layer * (2 * USES) + 2 * USE_MEM + 2)
                group(layer, K1_AT, K_EV, mem_hi, mem_lo)
                operand(layer, USE_Y)
                pe.wait_ge(act_evac, layer * ACT_EVS + K_EV + 4 + RING)
                x_group(layer, OUT_AT, 0)
                x_mean_square(layer, SUM_OUT, 0)
                pe.wait_ge(dve_evac, layer * DVE_EVS + OUT_SLABS + RING)
                group(layer, K2_AT, K_EV + 4, mem_hi, mem_lo)
                operand(layer, USE_XATTN)
                project(layer, Q_AT, Q_SLABS, act_evac, Q_EV, ACT_EVS)
                pe.wait_ge(act_evac, layer * ACT_EVS + PQ_EV + RING)
                for b in range(TB):
                    for h in range(XH):
                        for c in range(2):
                            last = nc.tensor.matmul(pair(4, 8)[:, b * XH + h, :], qT[:, 2 * h + c, b * P:(b + 1) * P],
                                                    kT[:, 2 * h + c, :], start=(c == 0), stop=(c == 1))
                    last.then_inc(xs_mm, 1)

                def memory_values(n):
                    pe.wait_ge(lo_ready, layer * SLABS + XV_AT + n + 1)
                    for half in range(2):
                        for b in range(2):
                            for i, (w, a) in enumerate(((w_hi, mem_hi), (w_lo, mem_hi), (w_hi, mem_lo))):
                                last = nc.tensor.matmul(ps[:, 2 * b + half, :], a[:, n, b * P:(b + 1) * P],
                                                        w[:, n % RING, 4 * half:4 * half + 4, :].rearrange("p k c -> p (k c)"),
                                                        start=(n == 0 and i == 0), stop=(n == KB - 1 and i == 2))
                        if n == KB - 1 and half == 0:
                            last.then_inc(vmem_mm, 1)
                    last.then_inc(slab_done, 1)

                for n in range(4):
                    memory_values(n)
                pe.wait_ge(prob_ready, layer * TB + TB)
                for mb in range(2):
                    for h in range(XH):
                        for b in range(TB):
                            last = nc.tensor.transpose(pair(4 + 2 * mb, 4)[:, h, b * P:(b + 1) * P],
                                                       prob[:, b * XH + h, mb * P:(mb + 1) * P], ident[:])
                last.then_inc(pt_mm, 1)
                for n in range(4, KB):
                    memory_values(n)
                pe.wait_ge(pt_dve, layer + 1)
                pe.wait_ge(pt_act, layer + 1)
                for half in range(2):
                    pe.wait_ge(vmem_dve, layer * 2 + half + 1)
                    pe.wait_ge(vmem_act, layer * 2 + half + 1)
                    for c in range(4 * half, 4 * half + 4):
                        for mb in range(2):
                            last = nc.tensor.matmul(pair(4, 8)[:, c, :], v_mem[:, mb, c * P:(c + 1) * P],
                                                    probT[:, mb, c // 2, :], start=(mb == 0), stop=(mb == 1))
                    last.then_inc(xo_mm, 1)

                def ao_half(k):
                    if k % 4 == 0:
                        pe.wait_ge(act_ready, layer * (2 * USES) + 2 * USE_AO + k // 4 + 1)

                x_group(layer, XO_AT, OUT_SLABS, ao_half)
                pe.wait_ge(dve_evac, (layer + 1) * DVE_EVS + RING)

                def pre_chunk(k):
                    if k == KB - 1:
                        x_mean_square(layer, SUM_XO, OUT_SLABS)
                    pe.wait_ge(pre_ready, layer * (2 * KB) + PRE_FFN * KB + k + 1)

                group(layer, PQ_AT, PQ_EV, pre_hi, pre_lo, before=pre_chunk)
                group(layer, PQ_AT + RING, PQ_EV + RING, pre_hi, pre_lo)
                operand(layer, USE_FFN)
                project(layer, PQ_AT + 2 * RING, PQ_SLABS - 2 * RING, act_evac, PQ_EV + 2 * RING, ACT_EVS)
                pe.wait_ge(act_evac, layer * ACT_EVS + U_EV + RING)
                pe.wait_ge(keys_loaded, layer * 16 + 16)
                pe.wait_ge(scaled, layer * 2 + 2)

                def scores(b):
                    for n in range(SETS):
                        last = nc.tensor.matmul(ps[:, 4 + n // 4, (n % 4) * P:(n % 4 + 1) * P],
                                                qpT[:, n, b * P:(b + 1) * P], skT[:, n, :], start=True, stop=True)
                    last.then_inc(sc_mm, 1)

                scores(0)
                project(layer, U_AT, RING, act_evac, U_EV, ACT_EVS)
                pe.wait_ge(sc_evac, layer * TB + 1)
                scores(1)
                project(layer, U_AT + RING, RETRIEVED - RING, act_evac, U_EV + RING, ACT_EVS)
                pe.wait_ge(decoded, layer + 1)
                for i, src in enumerate((row_f[:], col_f[:], g_exp[:].rearrange("p c k -> p (c k)"))):
                    for b in range(TB):
                        last = nc.tensor.transpose(ps[:, 4 + i // 2, (i % 2) * T + b * P:(i % 2) * T + (b + 1) * P],
                                                   src[:, b * P:(b + 1) * P], ident[:])
                last.then_inc(ret_mm, 1)
                project(layer, U_AT + RETRIEVED, U_SLABS - RETRIEVED, act_evac, U_EV + RETRIEVED, ACT_EVS)

                with pe.Fori(0, GROUPS // RING) as g:
                    for s in range(RING):
                        n = g * RING + s
                        pe.wait_ge(hot_act_ready if s in ACT_SLOTS else hot_col_ready,
                                   layer * (GROUPS // 2) + g * 2 + s // 2 + 1)
                        pe.wait_ge(hot_row_ready, layer * GROUPS + n + 1)
                        for i in range(4):
                            last = nc.tensor.matmul(ps[:, 4 + s, i * P:(i + 1) * P], hot_col[:, s, i, :],
                                                    hot_row[:, s, i, :], start=True, stop=True)
                        last.then_inc(gate_mm, 1)

                def expert_out(n, j, first=False, final=False):
                    pe.wait_ge(lo_ready, layer * SLABS + V_AT + n + 1)
                    pe.wait_ge(ga_ready, layer * V_SLABS + n + 1)
                    for half in range(2):
                        for b in range(TB):
                            for i, (w, a) in enumerate(PARTS):
                                last = nc.tensor.matmul(ps[:, 2 * b + half, :], a[:, j, b * P:(b + 1) * P],
                                                        w[:, j, 4 * half:4 * half + 4, :].rearrange("p k c -> p (k c)"),
                                                        start=(first and i == 0), stop=(final and i == 2))
                            if final and half + b < 2:
                                last.then_inc(y_done, 1)
                    last.then_inc(slab_done, 1)

                pe.wait_ge(act_evac, (layer + 1) * ACT_EVS + RING)
                for j in range(RING):
                    expert_out(j, j, first=(j == 0))
                with pe.Fori(1, V_SLABS // RING - 1) as g:
                    for j in range(RING):
                        expert_out(g * RING + j, j)
                for j in range(RING):
                    expert_out(V_SLABS - RING + j, j, final=(j == RING - 1))
                for half in range(2):
                    for b in range(TB):
                        pe.wait_ge((y_ready, y_act_ready)[b], layer * 2 + half + 1)
                        for c in range(4):
                            last = nc.tensor.transpose(pair(4, 8)[:, 4 * half + c, b * P:(b + 1) * P],
                                                       y_nat[b][:, half, c * P:(c + 1) * P], ident[:])
                    last.then_inc(y_mm, 1)
            for k in range(KB):
                pe.wait_ge(sq_chunk, DEPTH * CHUNKED + k + 1)
                last = nc.tensor.matmul(ps[:, 0, 0:T], ones[:], sq[:, k, :], start=(k == 0), stop=(k == KB - 1))
            last.then_inc(ms_ready, 1)



def kernel(x, mem, g_mix, w_in, b_if, conv_w, conv_b, g_head, w_out, g_xattn, g_mem,
           w_xq, w_xk, w_xv, w_xo, g_ffn, w_pq, sub_keys, u_experts, v_experts, g_final):
    import numpy as np
    import concourse.bacc as bacc
    from concourse.bass_utils import run_bass_kernel_spmd

    def col(a):
        return np.asarray(a).reshape(DEPTH, -1, P).transpose(0, 2, 1)

    def slab(w):
        w = np.asarray(w)
        return w.reshape(DEPTH, KB, P, -1, P).transpose(0, 3, 2, 1, 4).reshape(DEPTH, -1, P, D)

    w_in = np.asarray(w_in)
    cols = IN_SLABS * P
    z, k = slab(w_in[:, :, :cols]), slab(w_xk)
    parts = [z[:, at:at + 4] for at in Z_ORDER]
    parts += [k[:, 0:4], slab(w_out), k[:, 4:8], slab(w_xq), np.asarray(w_xv).reshape(DEPTH, KB, P, D),
              slab(w_xo), slab(w_pq),
             np.asarray(u_experts).reshape(DEPTH, NKEYS, NKEYS, KB, P).transpose(0, 1, 4, 3, 2).reshape(DEPTH, NKEYS, P, D),
             np.asarray(v_experts).reshape(DEPTH, NKEYS, P, D)]
    slabs = np.concatenate(parts, axis=1).reshape(DEPTH * SLABS, P, D)
    w_if = w_in[:, :, cols:].reshape(DEPTH, KB, P, 8).transpose(0, 2, 1, 3).reshape(DEPTH, P, KB * 8)
    cw = np.asarray(conv_w)
    params = np.zeros((DEPTH + 1, P, N_PARAM), np.float32)
    params[DEPTH, :, G_MIX:G_MIX + KB] = np.asarray(g_final).reshape(KB, P).T
    params[:DEPTH] = np.concatenate([col(g_mix), col(g_mem), col(g_xattn), col(g_ffn), col(g_head),
                             col(cw.reshape(DEPTH, -1)), col(conv_b),
                             np.broadcast_to(np.asarray(b_if)[:, None, :], (DEPTH, P, 8)), w_if], axis=2)
    arrays = {
        "x": np.asarray(x)[0].reshape(T, KB, P).transpose(2, 1, 0),
        "mem": np.asarray(mem)[0].reshape(NMEM, KB, P).transpose(2, 1, 0),
        "slabs": slabs,
        "params": params,
        "sub_keys": np.asarray(sub_keys).reshape(DEPTH, SETS, NKEYS, P).transpose(0, 3, 1, 2),
    }
    arrays = {name: np.ascontiguousarray(a) for name, a in arrays.items()}
    nc = bacc.Bacc("TRN2", target_bir_lowering=False, num_devices=1)
    args = [nc.dram_tensor(name, a.shape, FP32, kind="ExternalInput").ap() for name, a in arrays.items()]
    out = nc.dram_tensor("out", (P, KB, T), FP32, kind="ExternalOutput").ap()
    trunk(nc, *args, out)
    got = run_bass_kernel_spmd(nc, [arrays], core_ids=[0]).results[0]["out"]
    return got.transpose(2, 1, 0).reshape(1, T, D)
```
